# Optimizing a Trainium2 kernel written in Bass

```python
import jax, jax.numpy as jnp
from jax import lax
import numpy as np

D_MODEL = 1024
BATCH = 1
SEQ = 512
DEPTH = 2

CTX_LEN = 256
GRID_W = 64
HEAD_DIM = 64
A_HEADS = 6
A_KV_HEADS = 2
B_HEADS = 6
B_KV_HEADS = 2
C_GROUPS = 4
C_GROUP_DIM = 64
A_Q = A_HEADS * HEAD_DIM
A_KV = A_KV_HEADS * HEAD_DIM
B_Q = B_HEADS * HEAD_DIM
B_KV = B_KV_HEADS * HEAD_DIM
C_WIDTH = C_GROUPS * C_GROUP_DIM
MIX_WIDTH = A_Q + B_Q + C_WIDTH
D_IN = A_Q + 2 * A_KV + B_Q + 2 * B_KV + C_WIDTH
WINDOW = 128
BLOCK = 128
D_FF = 2816
ROPE_THETA = 10000.0
NORM_EPS = 1e-6
N_MOD = 9
NEG_INF = -1e30

kernel_name = "hybrid_window_axial_fourier_macaron_dit"

def rms_norm(x, g):
    xf = x.astype(jnp.float32)
    y = xf * lax.rsqrt(jnp.mean(xf * xf, axis=-1, keepdims=True) + NORM_EPS)
    return (y * g.astype(jnp.float32)).astype(x.dtype)

def modulate(x, shift, scale):
    return x * (1 + scale) + shift

def swiglu(x, w_gate, w_up, w_down):
    return (jax.nn.silu(x @ w_gate) * (x @ w_up)) @ w_down

def axial_rope_angles(length):
    t = jnp.arange(length)
    row = (t // GRID_W).astype(jnp.float32)
    col = (t % GRID_W).astype(jnp.float32)
    half = HEAD_DIM // 2
    inv = ROPE_THETA ** (-jnp.arange(0, half, 2, dtype=jnp.float32) / half)
    return row[:, None] * inv, col[:, None] * inv

def _rotate_half(x, ang):
    n2 = x.shape[-1] // 2
    cos = jnp.cos(ang)[:, None, :]
    sin = jnp.sin(ang)[:, None, :]
    x1, x2 = x[..., :n2], x[..., n2:]
    return jnp.concatenate([x1 * cos - x2 * sin, x2 * cos + x1 * sin], axis=-1)

def apply_axial_rope(x, ang_row, ang_col):
    xf = x.astype(jnp.float32)
    half = HEAD_DIM // 2
    out = jnp.concatenate([_rotate_half(xf[..., :half], ang_row),
                           _rotate_half(xf[..., half:], ang_col)], axis=-1)
    return out.astype(x.dtype)

def split_mixer_inputs(u):
    bn, length = u.shape[:2]
    sizes = (A_Q, A_KV, A_KV, B_Q, B_KV, B_KV, C_WIDTH)
    idx = [int(i) for i in np.cumsum(sizes)[:-1]]
    qa, ka, va, qb, kb, vb, uf = jnp.split(u, idx, axis=-1)
    heads = lambda t: t.reshape(bn, length, -1, HEAD_DIM)
    return heads(qa), heads(ka), heads(va), heads(qb), heads(kb), heads(vb), uf

def window_attention_latent(q, k, v, k_ctx, v_ctx, sink):
    bn, length = q.shape[:2]
    nb = length // BLOCK
    g = A_HEADS // A_KV_HEADS
    span = BLOCK + 2 * WINDOW
    scale = HEAD_DIM ** -0.5
    qb = q.reshape(bn, nb, BLOCK, A_KV_HEADS, g, HEAD_DIM)
    pad = ((0, 0), (WINDOW, WINDOW), (0, 0), (0, 0))
    kp, vp = jnp.pad(k, pad), jnp.pad(v, pad)

    def band(t):
        return jnp.concatenate(
            [t[:, s:s + length].reshape(bn, nb, BLOCK, A_KV_HEADS, HEAD_DIM) for s in (0, BLOCK, 2 * BLOCK)],
            axis=2)

    kb, vb = band(kp), band(vp)
    s_band = jnp.einsum('bnqkgd,bnskd->bnkgqs', qb, kb, preferred_element_type=jnp.float32) * scale
    s_ctx = jnp.einsum('bnqkgd,bskd->bnkgqs', qb, k_ctx, preferred_element_type=jnp.float32) * scale
    qpos = jnp.arange(nb)[:, None, None] * BLOCK + jnp.arange(BLOCK)[None, :, None]
    kpos = jnp.arange(nb)[:, None, None] * BLOCK - WINDOW + jnp.arange(span)[None, None, :]
    valid = (jnp.abs(kpos - qpos) <= WINDOW) & (kpos >= 0) & (kpos < length)
    s_band = jnp.where(valid[None, :, None, None], s_band, NEG_INF)
    sink_l = jnp.broadcast_to(sink.astype(jnp.float32).reshape(1, 1, A_KV_HEADS, g, 1, 1),
                              s_band.shape[:-1] + (1,))
    p = jax.nn.softmax(jnp.concatenate([s_band, s_ctx, sink_l], axis=-1), axis=-1)
    lc = k_ctx.shape[1]
    p_band = p[..., :span].astype(v.dtype)
    p_ctx = p[..., span:span + lc].astype(v.dtype)
    o = (jnp.einsum('bnkgqs,bnskd->bnqkgd', p_band, vb)
         + jnp.einsum('bnkgqs,bskd->bnqkgd', p_ctx, v_ctx))
    return o.reshape(bn, length, A_Q)

def global_attention_latent(q, k, v, k_ctx, v_ctx):
    bn, length = q.shape[:2]
    nb = length // BLOCK
    g = B_HEADS // B_KV_HEADS
    scale = HEAD_DIM ** -0.5
    qb = q.reshape(bn, nb, BLOCK, B_KV_HEADS, g, HEAD_DIM).transpose(1, 0, 2, 3, 4, 5)

    def one_block(qblk):
        s_lat = jnp.einsum('bqkgd,bskd->bkgqs', qblk, k, preferred_element_type=jnp.float32) * scale
        s_ctx = jnp.einsum('bqkgd,bskd->bkgqs', qblk, k_ctx, preferred_element_type=jnp.float32) * scale
        p = jax.nn.softmax(jnp.concatenate([s_lat, s_ctx], axis=-1), axis=-1).astype(v.dtype)
        return (jnp.einsum('bkgqs,bskd->bqkgd', p[..., :length], v)
                + jnp.einsum('bkgqs,bskd->bqkgd', p[..., length:], v_ctx))

    o = lax.map(one_block, qb)
    return o.transpose(1, 0, 2, 3, 4, 5).reshape(bn, length, B_Q)

def ctx_attention(q, k, v, sink=None):
    bn, lc, hq, _ = q.shape
    hk = k.shape[2]
    g = hq // hk
    qg = q.reshape(bn, lc, hk, g, HEAD_DIM)
    s = jnp.einsum('bqkgd,bskd->bkgqs', qg, k, preferred_element_type=jnp.float32) * (HEAD_DIM ** -0.5)
    if sink is not None:
        sink_l = jnp.broadcast_to(sink.astype(jnp.float32).reshape(1, hk, g, 1, 1), s.shape[:-1] + (1,))
        s = jnp.concatenate([s, sink_l], axis=-1)
    p = jax.nn.softmax(s, axis=-1)[..., :lc].astype(v.dtype)
    o = jnp.einsum('bkgqs,bskd->bqkgd', p, v)
    return o.reshape(bn, lc, hq * HEAD_DIM)

def fourier_mix(u, w_four):
    bn, length = u.shape[:2]
    ug = u.astype(jnp.float32).reshape(bn, length, C_GROUPS, C_GROUP_DIM)
    f = jnp.fft.fft2(ug, axes=(1, 3), norm='ortho').real.astype(u.dtype)
    return jnp.einsum('blgc,gcd->blgd', f, w_four).reshape(bn, length, C_WIDTH)

def trunk_layer(h, hc, c, c_ctx, p, ang_row, ang_col, update_ctx):
    mod = (jax.nn.silu(c) @ p['w_ada'] + p['b_ada'])[:, None, :]
    mod_c = jax.nn.silu(c_ctx) @ p['w_ada'] + p['b_ada']
    s1, sc1, g1, s2, sc2, g2, s3, sc3, g3 = jnp.split(mod, N_MOD, axis=-1)
    s1c, sc1c, g1c, s2c, sc2c, g2c, s3c, sc3c, g3c = jnp.split(mod_c, N_MOD, axis=-1)

    h = h + 0.5 * g1 * swiglu(modulate(rms_norm(h, p['g_ffn1']), s1, sc1), p['w1_gate'], p['w1_up'], p['w1_down'])
    hc = hc + 0.5 * g1c * swiglu(modulate(rms_norm(hc, p['g_ffn1']), s1c, sc1c), p['w1_gate'], p['w1_up'], p['w1_down'])

    qa, ka, va, qb, kb, vb, uf = split_mixer_inputs(modulate(rms_norm(h, p['g_mix']), s2, sc2) @ p['w_in'])
    qa_c, ka_c, va_c, qb_c, kb_c, vb_c, uf_c = split_mixer_inputs(
        modulate(rms_norm(hc, p['g_mix']), s2c, sc2c) @ p['w_in'])
    qb, kb = rms_norm(qb, p['g_qn']), rms_norm(kb, p['g_kn'])
    qb_c, kb_c = rms_norm(qb_c, p['g_qn']), rms_norm(kb_c, p['g_kn'])
    qa, ka = apply_axial_rope(qa, ang_row, ang_col), apply_axial_rope(ka, ang_row, ang_col)
    qb, kb = apply_axial_rope(qb, ang_row, ang_col), apply_axial_rope(kb, ang_row, ang_col)

    o = jnp.concatenate([
        window_attention_latent(qa, ka, va, ka_c, va_c, p['sink']),
        global_attention_latent(qb, kb, vb, kb_c, vb_c),
        fourier_mix(uf, p['w_four']),
    ], axis=-1) @ p['w_out']
    h = h + g2 * o

    h = h + 0.5 * g3 * swiglu(modulate(rms_norm(h, p['g_ffn2']), s3, sc3), p['w2_gate'], p['w2_up'], p['w2_down'])

    if update_ctx:
        oc = jnp.concatenate([
            ctx_attention(qa_c, ka_c, va_c, p['sink']),
            ctx_attention(qb_c, kb_c, vb_c),
            fourier_mix(uf_c, p['w_four']),
        ], axis=-1) @ p['w_out']
        hc = hc + g2c * oc
        hc = hc + 0.5 * g3c * swiglu(modulate(rms_norm(hc, p['g_ffn2']), s3c, sc3c),
                                     p['w2_gate'], p['w2_up'], p['w2_down'])
    return h, hc

def setup_inputs(seed: int = 0) -> dict:
    key = jax.random.key(seed)
    ks = jax.random.split(key, 24)
    f32 = jnp.float32
    nrm = lambda k, shape, s: jax.random.normal(k, shape, f32) * s
    gain = lambda k, shape: 1.0 + 0.02 * jax.random.normal(k, shape, f32)
    D, L = DEPTH, D_MODEL
    return {
        'x': nrm(ks[0], (BATCH, SEQ, D_MODEL), 1.0),
        'c': nrm(ks[1], (BATCH, D_MODEL), 1.0),
        'ctx': nrm(ks[2], (BATCH, CTX_LEN, D_MODEL), 1.0),
        'c_ctx': nrm(ks[3], (D_MODEL,), 1.0),
        'w_ada': nrm(ks[4], (D, L, N_MOD * L), 0.5 * L ** -0.5),
        'b_ada': nrm(ks[5], (D, N_MOD * L), 0.01),
        'g_ffn1': gain(ks[6], (D, L)),
        'g_mix': gain(ks[7], (D, L)),
        'g_ffn2': gain(ks[8], (D, L)),
        'w_in': nrm(ks[9], (D, L, D_IN), L ** -0.5),
        'g_qn': gain(ks[10], (D, HEAD_DIM)),
        'g_kn': gain(ks[11], (D, HEAD_DIM)),
        'sink': nrm(ks[12], (D, A_HEADS), 0.5),
        'w_four': nrm(ks[13], (D, C_GROUPS, C_GROUP_DIM, C_GROUP_DIM), C_GROUP_DIM ** -0.5),
        'w_out': nrm(ks[14], (D, MIX_WIDTH, L), MIX_WIDTH ** -0.5),
        'w1_gate': nrm(ks[15], (D, L, D_FF), L ** -0.5),
        'w1_up': nrm(ks[16], (D, L, D_FF), L ** -0.5),
        'w1_down': nrm(ks[17], (D, D_FF, L), D_FF ** -0.5),
        'w2_gate': nrm(ks[18], (D, L, D_FF), L ** -0.5),
        'w2_up': nrm(ks[19], (D, L, D_FF), L ** -0.5),
        'w2_down': nrm(ks[20], (D, D_FF, L), D_FF ** -0.5),
        'g_final': gain(ks[21], (L,)),
    }

def reference(x, c, ctx, c_ctx, w_ada, b_ada, g_ffn1, g_mix, g_ffn2, w_in, g_qn, g_kn, sink, w_four,
              w_out, w1_gate, w1_up, w1_down, w2_gate, w2_up, w2_down, g_final):
    length = x.shape[1]
    ang_row, ang_col = axial_rope_angles(length)
    h, hc = x, ctx
    for l in range(DEPTH):
        p = {
            'w_ada': w_ada[l], 'b_ada': b_ada[l], 'g_ffn1': g_ffn1[l], 'g_mix': g_mix[l], 'g_ffn2': g_ffn2[l],
            'w_in': w_in[l], 'g_qn': g_qn[l], 'g_kn': g_kn[l], 'sink': sink[l], 'w_four': w_four[l],
            'w_out': w_out[l], 'w1_gate': w1_gate[l], 'w1_up': w1_up[l], 'w1_down': w1_down[l],
            'w2_gate': w2_gate[l], 'w2_up': w2_up[l], 'w2_down': w2_down[l],
        }
        h, hc = trunk_layer(h, hc, c, c_ctx, p, ang_row, ang_col, update_ctx=(l < DEPTH - 1))
    return rms_norm(h, g_final)


_drawn_inputs = setup_inputs


def setup_inputs(seed=0):
    import zlib

    import numpy as np

    out = dict(_drawn_inputs(seed))
    spreads = {}
    factors = {'ctx': 2.857,
     'b_ada': 5.073,
     'g_ffn1': 8.0,
     'g_mix': 8.0,
     'g_ffn2': 8.0,
     'g_qn': 8.0,
     'g_kn': 8.0,
     'sink': 8.0,
     'g_final': 2.748}
    for name, (base, spread) in spreads.items():
        noise = np.random.default_rng([zlib.crc32(name.encode()), seed]).standard_normal(out[name].shape)
        drawn = base * np.exp(spread * noise) if base else spread * noise
        out[name] = __import__('jax').numpy.asarray(drawn.astype(out[name].dtype))
    for name, factor in factors.items():
        out[name] = (out[name] * factor).astype(out[name].dtype)
    return out
```

```python
from contextlib import ExitStack

import numpy as np
import concourse.bass as bass
from concourse import mybir

F32 = mybir.dt.float32
F32R = mybir.dt.float32r
BF16 = mybir.dt.bfloat16
ALU = mybir.AluOpType
ACT = mybir.ActivationFunctionType
AX = mybir.AxisListType

P = 128
D_MODEL, SEQ, CTX, DEPTH, D_FF = 1024, 512, 256, 2, 2816
GRID_W, HD, N_MOD = 64, 64, 9
NORM_EPS, NEG_INF, ROPE_THETA = 1e-6, -1e30, 10000.0
TOK = SEQ + CTX
KD = D_MODEL // P
NF = D_FF // P
GROUPS = 2
GF = NF // GROUPS
W_IN_TILES, W_OUT_TILES = 12, 8
FFN_TILES = 2 * NF + GROUPS * KD
SCALE = float(HD) ** -0.5
ADA_COLS = 384
ADA_UNITS = N_MOD * D_MODEL // ADA_COLS
UNITS_PER_STAGE = ADA_UNITS // 3
UC = ADA_COLS // P
MODC = N_MOD * KD

UF, VA, VB, KA, QA, KB, QB = (0, 1), 2, 3, 4, (5, 6, 7), 8, (9, 10, 11)
ROPED = range(4, 12)


def w_in_width(layer, j):
    return TOK if layer < DEPTH - 1 or j in (VA, VB, KA, KB) else SEQ


def spans(width):
    return [(0, SEQ), (SEQ, TOK)] if width == TOK else [(0, SEQ)]


class Plan:

    def __init__(self):
        self.stages = []
        t = r = resid = 0
        self.release = []
        pairs = scores = 0
        for layer in range(DEPTH):
            last = layer == DEPTH - 1
            for kind in ("ffn1", "mix", "ffn2"):
                width = SEQ if last and kind == "ffn2" else TOK
                s = dict(kind=kind, layer=layer, n=len(self.stages), t=t, r=r, resid=resid, pairs=pairs,
                         width=width, out_width=width if kind != "mix" or not last else SEQ, scores=scores)
                self.stages.append(s)
                if kind == "mix":
                    for j in range(W_IN_TILES):
                        self.release.append(("evac_done", W_IN_TILES * layer + j + 1))
                    s["tiles"] = score_tiles(layer)
                    for i in range(len(s["tiles"])):
                        self.release.append(("exp_done", scores + i + 1))
                    scores += len(s["tiles"])
                    for d in range(KD):
                        self.release.append(("resid_done", resid + d + 1))
                    resid += KD
                    t += W_IN_TILES + W_OUT_TILES
                    r += W_IN_TILES + len(s["tiles"]) + W_OUT_TILES
                else:
                    for g in range(GROUPS):
                        for f in range(GF):
                            self.release.append(("silu_done", pairs + 1))
                            self.release.append(("prod_done", pairs + 1))
                            pairs += 1
                        for d in range(KD):
                            self.release.append(("resid_done", resid + 1))
                            resid += 1
                    t += FFN_TILES
                    r += FFN_TILES
        self.ada = {(0, 0): 8, (0, 1): 16, (2, 0): 24, (2, 1): 32, (3, 0): 40}


def score_tiles(layer):
    blocks = 6 if layer < DEPTH - 1 else 4
    return [(b, kv, q, g) for b in range(2) for kv in range(2) for q in range(blocks) for g in range(3)]


def key_blocks(branch, q):
    if q >= 4:
        return []
    return list(range(max(0, q - 1), min(3, q + 1) + 1)) if branch == 0 else [0, 1, 2, 3]


def build(nc, x_t, ctx_t, c_cols, w_ada, b_ada, gains, g_final, qk_gain, sink, w_in, w_four, w_out,
          w_gu, w_down, rope, dft_chan, dft_lat, dft_ctx, out):
    plan = Plan()
    stages = plan.stages
    ctx = ExitStack()
    with ctx:
        sem_of = {}

        def sem(name):
            sem_of[name] = ctx.enter_context(nc.semaphore(name))
            return sem_of[name]

        at = [nc.sbuf_base + 31 & ~31]

        def sb(name, shape, dt=F32, offset=None):
            size = int(np.prod(shape[1:])) * (2 if dt == BF16 else 4)
            if offset is None:
                offset = at[0]
                at[0] += size + 31 & ~31
            return nc.alloc_sbuf_tensor_at(name, shape, dt, offset=offset)

        h = sb("h", [P, KD, TOK])
        xh = sb("xh", [P, KD, TOK], F32R)
        xl = sb("xl", [P, KD, TOK], F32R)
        raw = sb("raw", [P, 2, GF * P])
        whi = sb("whi", [P, 2, GF * P], F32R)
        wlo = sb("wlo", [P, 2, GF * P], F32R)
        ones = sb("ones", [P, P])
        head_ones = sb("head_ones", [P, P])
        ident = sb("ident", [P, P])
        ident_b = sb("ident_b", [P, P], BF16)
        band_mask = sb("band_mask", [P, 2, P], BF16)
        chan = sb("chan", [P, 2, P])
        modv = sb("modv", [P, 2, DEPTH * MODC])
        bias_ada = sb("bias_ada", [P, DEPTH * MODC])
        gain = sb("gain", [P, DEPTH * 3, KD])
        gain_final = sb("gain_final", [P, KD])
        qkg = sb("qkg", [P, DEPTH * 2])
        sinks = sb("sinks", [P, DEPTH * 6])
        sinks8 = sb("sinks8", [P, DEPTH * 6])
        cond = sb("cond", [P, 2, KD])
        scond = sb("scond", [P, 2, KD])
        eps = sb("eps", [P, 1])
        ada_sum = sb("ada_sum", [P, 2, UC])
        vec_scale = sb("vec_scale", [P, 2, KD])
        vec_gate = sb("vec_gate", [P, 2, KD])
        row_max = sb("row_max", [P, 2])
        neg_max = sb("neg_max", [P, 4])
        row_sum = sb("row_sum", [P, 4])
        sink_exp = sb("sink_exp", [P, 4])
        row_tot = sb("row_tot", [P, 2])
        row_inv = sb("row_inv", [P, 4])
        acc = sb("acc", [P, TOK])
        rstd = sb("rstd", [P, TOK])
        work = at[0]
        room = nc.sbuf_usable_end - work

        ah = sb("ah", [P, GF, TOK], F32R, work)
        al = sb("al", [P, GF, TOK], F32R, work + 33792)
        sil = sb("sil", [P, TOK], F32, work + 67584)
        atmp = sb("atmp", [P, TOK], F32, work + 70656)
        sq = sb("sq", [P, 2, TOK], F32, work + 67584)
        ada_buf = sb("ada_buf", [P, KD, ADA_COLS], F32, work + 73728)
        ada_acc = sb("ada_acc", [P, 2, ADA_COLS], F32, work + 86016)
        ada_tmp = sb("ada_tmp", [P, 2, ADA_COLS], F32, work + 89088)
        assert room >= 92160, room
        ada_first = [sb(f"ada_first{i}", [P, KD, ADA_COLS], F32, work + 12288 * i) for i in range(4)]
        t1 = sb("t1", [P, 2, TOK], F32, work + 49152)
        t2 = sb("t2", [P, 2, TOK], F32, work + 55296)
        v2 = sb("v2", [P, 2, 6, 2 * P], F32R, work)
        un = sb("un", [P, 2, TOK], F32, work + 12288)
        rot = sb("rot", [P, 2, SEQ], F32, work + 18432)
        ucos = sb("ucos", [P, 2, SEQ], F32, work + 22528)
        roped = sb("roped", [P, 2, TOK], F32, work + 26624)
        qkh = sb("qkh", [P, 2, TOK], F32R, work + 32768)
        qkl = sb("qkl", [P, 2, TOK], F32R, work + 38912)
        uf = sb("uf", [P, 2, TOK], F32, work + 45056)
        rope_tab = sb("rope_tab", [P, 2, SEQ], F32, work + 51200)
        pos_lat = sb("pos_lat", [P, 2, 4, SEQ], F32, work + 55296)
        pos_ctx = sb("pos_ctx", [P, 2, 2, CTX], F32, work + 71680)
        v1 = sb("v1", [P, 6, 2, 2 * P], F32, work + 75776)
        four = sb("four", [P, 2, 2 * P], F32, work + 88064)
        wf = sb("wf", [P, 2, P], F32, work + 90112)
        pth = sb("pth", [P, 2, 6, 3 * P], F32R, work + 12288)
        ptl = sb("ptl", [P, 2, 6, 3 * P], F32R, work + 30720)
        corr = sb("corr", [P, 2, 3 * P], F32, work + 49152)
        osum = sb("osum", [P, 2, 3 * P], F32, work + 52224)
        k2 = sb("k2", [P, 2, 2, TOK], F32R, work + 55296)
        q2 = sb("q2", [P, 2, 3, TOK], F32R, work + 67584)
        prob = sb("prob", [P, 2, TOK], F32, work + 86016)

        scratch = nc.dram_tensor("qk_parts", [8, 2, P, TOK], F32).ap()

        ring = [ctx.enter_context(nc.psum_tensor(f"ring{i}", [P, 1024], F32)) for i in range(2)]
        side = ctx.enter_context(nc.psum_tensor("side", [P, 1024], F32))
        bank = [ctx.enter_context(nc.psum_tensor(f"bank{i}", [P, 512], F32)) for i in range(2)]

        const_loaded = sem("const_loaded")
        h_loaded = sem("h_loaded")
        w_loaded = [sem("w_loaded_even"), sem("w_loaded_odd")]
        whi_ready, wlo_ready, mm_done = sem("whi_ready"), sem("wlo_ready"), sem("mm_done")
        consts_ready = sem("consts_ready")
        cond_ready, sink_ready = sem("cond_ready"), sem("sink_ready")
        ada_first_loaded = [sem(f"ada_first_loaded{i}") for i in range(4)]
        ada_loaded = sem("ada_loaded")
        ada_lat_done, ada_prod_done, ada_ctx_done = sem("ada_lat_done"), sem("ada_prod_done"), sem("ada_ctx_done")
        ada_turned, ada_red_done = sem("ada_turned"), sem("ada_red_done")
        silu_done, prod_done, ahi_done, alo_done = sem("silu_done"), sem("prod_done"), sem("ahi_done"), sem("alo_done")
        resid_done, sq_done, acc_done, ssq_ready = sem("resid_done"), sem("sq_done"), sem("acc_done"), sem("ssq_ready")
        std_done, rstd_ready, vec_ready = sem("std_done"), sem("rstd_ready"), sem("vec_ready")
        t1_ready, mod_done, x_ready = sem("t1_ready"), sem("mod_done"), sem("x_ready")
        tab_loaded, wf_zeroed, wf_loaded = sem("tab_loaded"), sem("wf_zeroed"), sem("wf_loaded")
        evac_done, four_mm, four_ready = sem("evac_done"), sem("four_mm"), sem("four_ready")
        v_turned, vhi_done, v_ready = sem("v_turned"), sem("vhi_done"), sem("v_ready")
        f1_done, v1_even, v1_odd = sem("f1_done"), sem("v1_even"), sem("v1_odd")
        f2_done, f2_read = sem("f2_done"), sem("f2_read")
        bn_done, bstd_done, brstd_done, unorm_done = sem("bn_done"), sem("bstd_done"), sem("brstd_done"), sem("unorm_done")
        sqh_done, rot_done, rope_done, qhi_done, qlo_done = sem("sqh_done"), sem("rot_done"), sem("rope_done"), sem("qhi_done"), sem("qlo_done")
        stored = [sem("stored_even"), sem("stored_odd")]
        stack_loaded = [sem("stack_loaded_even"), sem("stack_loaded_odd")]
        sc_done, max_done, nm_ready, exp_done = sem("sc_done"), sem("max_done"), sem("nm_ready"), sem("exp_done")
        tot_done, inv_ready, pn_ready = sem("tot_done"), sem("inv_ready"), sem("pn_ready")
        sink_exp_done = sem("sink_exp_done")
        p_turned, pth_done, pt_ready, pv_done = sem("p_turned"), sem("pth_done"), sem("pt_ready"), sem("pv_done")
        corr_done, osum_done, ohi_done, mix_ready = sem("corr_done"), sem("osum_done"), sem("ohi_done"), sem("mix_ready")
        fhi_done = sem("fhi_done")
        out_ready, out_stored = sem("out_ready"), sem("out_stored")

        CONSTS = 11

        def slot_free(eng, r, i=None, first=0):
            if r < 2:
                return
            name, value = plan.release[r - 2]
            if i is None:
                eng.wait_ge(sem_of[name], value)
            else:
                step = plan.release[r][1] - value
                assert plan.release[r][0] == name
                eng.wait_ge(sem_of[name], (i - first) * step + value)

        def tile_sizes(s):
            return ([KD] * (W_IN_TILES + W_OUT_TILES) if s["kind"] == "mix"
                    else ([KD] * 2 * GF + [GF] * KD) * GROUPS)

        NK = [nk for s in stages for nk in tile_sizes(s)]
        N_TILES = len(NK)

        def mix_counts(layer):
            before = sum(2 + len(score_tiles(l)) // 3 for l in range(layer))
            per = len(score_tiles(layer)) // 6
            return before + 2, before + 2 + per, before + 2 + 2 * per

        block = ctx.enter_context(nc.Block())

        @block.sync
        def _(sp):
            sp.dma_start(cond[:], c_cols).then_inc(const_loaded, 16)
            sp.dma_start(bias_ada[:], b_ada).then_inc(const_loaded, 16)
            for u in range(UNITS_PER_STAGE):
                if u >= 4:
                    sp.wait_ge(ada_lat_done, KD * (u - 3))
                    sp.wait_ge(ada_prod_done, KD * (u - 3))
                sp.dma_start(ada_first[u % 4][:], w_ada[u]).then_inc(ada_first_loaded[u % 4], 16)
                if u == 0:
                    sp.dma_start(h[:, :, 0:SEQ], x_t).then_inc(h_loaded, 16)
                    sp.dma_start(h[:, :, SEQ:TOK], ctx_t).then_inc(h_loaded, 16)
                    for dst, src in ((gain, gains), (gain_final, g_final), (qkg, qk_gain), (sinks, sink),
                                     (chan, dft_chan)):
                        sp.dma_start(dst[:], src).then_inc(const_loaded, 16)

            def load_w(t, slot, src, nk):
                if not isinstance(t, int) or t >= 2:
                    sp.wait_ge(wlo_ready, t - 1)
                sp.dma_start(raw[:, slot, 0:nk * P], src).then_inc(w_loaded[slot], 16)

            def load_ada(u):
                sp.wait_ge(ada_lat_done, u * KD)
                sp.wait_ge(ada_prod_done, u * KD)
                sp.dma_start(ada_buf[:], w_ada[u]).then_inc(ada_loaded, 16)

            for s in stages:
                layer, n = s["layer"], s["n"]
                if s["kind"] == "mix":
                    load_w(s["t"], 0, w_in[layer, 0], KD)
                    load_w(s["t"] + 1, 1, w_in[layer, 1], KD)
                    sp.wait_ge(acc_done, KD * (n + 1))
                    sp.wait_ge(x_ready, KD * (n + 1))
                    sp.dma_start(rope_tab[:], rope).then_inc(tab_loaded, 16)
                    sp.dma_start(pos_lat[:], dft_lat).then_inc(tab_loaded, 16)
                    sp.dma_start(pos_ctx[:], dft_ctx).then_inc(tab_loaded, 16)
                    sp.wait_ge(wf_zeroed, layer + 1)
                    for g in range(4):
                        a = HD * (g % 2)
                        sp.dma_start(wf[a:a + HD, g // 2, a:a + HD], w_four[layer, g]).then_inc(wf_loaded, 16)

                    def store(q):
                        width = w_in_width(layer, ROPED[q])
                        sp.wait_ge(qlo_done, 8 * layer + q + 1)
                        sp.dma_start(scratch[q, 0, :, 0:width], qkh[:, q % 2, 0:width].bitcast(F32)).then_inc(stored[q % 2], 16)
                        sp.dma_start(scratch[q, 1, :, 0:width], qkl[:, q % 2, 0:width].bitcast(F32)).then_inc(stored[q % 2], 16)

                    def load_stack(z):
                        branch, kv, slot = z // 2, z % 2, z % 2
                        width = w_in_width(layer, QA[0])
                        sp.wait_ge(stored[0], 32 * (4 * layer + 2 * (branch + 1)))
                        sp.wait_ge(stored[1], 32 * (4 * layer + 2 * (branch + 1)))
                        if z >= 2:
                            sp.wait_ge(sc_done, s["scores"] + len(s["tiles"]) // 4 * (z - 1))
                        rows = slice(kv * HD, kv * HD + HD)
                        for half in range(2):
                            part = slice(half * HD, half * HD + HD)
                            sp.dma_start(k2[part, slot, :, :].bitcast(F32),
                                         scratch[4 * branch, :, rows, :].rearrange("x p c -> p x c")).then_inc(stack_loaded[slot], 16)
                            sp.dma_start(q2[part, slot, :, 0:width].bitcast(F32),
                                         scratch[4 * branch + 1:4 * branch + 4, half, rows, 0:width].rearrange("g p c -> p g c")).then_inc(stack_loaded[slot], 16)

                    for j in range(2, W_IN_TILES):
                        load_w(s["t"] + j, j % 2, w_in[layer, j], KD)
                        if j >= 8:
                            store(j - 8)
                    load_w(s["t"] + 12, 0, w_out[layer, 0], KD)
                    store(4)
                    sp.wait_ge(f2_done, 2 * (layer + 1))
                    load_stack(0)
                    load_stack(1)
                    load_w(s["t"] + 13, 1, w_out[layer, 1], KD)
                    store(5)
                    store(6)
                    store(7)
                    load_stack(2)
                    load_stack(3)
                    for d in range(2, W_OUT_TILES):
                        load_w(s["t"] + 12 + d, d % 2, w_out[layer, d], KD)
                    continue
                j = 2 * layer + (s["kind"] == "ffn2")
                for g in range(GROUPS):
                    t = s["t"] + g * (2 * GF + KD)
                    if t == 0:
                        for u in range(2):
                            load_w(u, u, w_gu[0, 0, u], KD)
                    with sp.Fori(1 if t == 0 else 0, GF) as i:
                        for u in range(2):
                            load_w(t + u + 2 * i, u, w_gu[j, g * GF + i, u], KD)
                    t += 2 * GF
                    u0 = plan.ada.get((n, g))
                    with sp.Fori(0, KD // 2) as i:
                        for u in range(2):
                            load_w(t + u + 2 * i, u, w_down[j, g, 2 * i + u], GF)
                            if u0 is not None:
                                load_ada(u0 + u + 2 * i)
            sp.wait_ge(stored[0], 32 * 4 * DEPTH)
            sp.wait_ge(stored[1], 32 * 4 * DEPTH)
            for d in range(KD):
                sp.wait_ge(out_ready, d + 1)
                sp.dma_start(out[:, d, :], h[:, d, 0:SEQ]).then_inc(out_stored, 16)
            sp.wait_ge(out_stored, 16 * KD)

        @block.gpsimd
        def _(pool):
            pool.memset(ones[:], 1.0).then_inc(consts_ready, 1)
            pool.memset(head_ones[:], 0.0).then_inc(consts_ready, 1)
            pool.memset(ident[:], 0.0).then_inc(consts_ready, 1)
            pool.memset(ident_b[:], 0.0).then_inc(consts_ready, 1)
            pool.memset(band_mask[:], 0.0).then_inc(consts_ready, 1)
            pool.memset(eps[:], NORM_EPS).then_inc(consts_ready, 1)
            pool.wait_ge(consts_ready, 6)
            pool.memset(head_ones[0:HD, 0:HD], 1.0).then_inc(consts_ready, 1)
            pool.wait_ge(consts_ready, 7)
            pool.memset(head_ones[HD:P, HD:P], 1.0).then_inc(consts_ready, 1)
            pool.wait_ge(consts_ready, 8)
            for m in (ident, ident_b):
                pool.affine_select(out=m[:], in_=m[:], compare_op=ALU.not_equal, fill=1.0, base=0,
                                   pattern=[[-1, P]], channel_multiplier=1).then_inc(consts_ready, 1)
            pool.affine_select(out=band_mask[:, 0], in_=band_mask[:, 0], compare_op=ALU.is_ge, fill=NEG_INF,
                               base=0, pattern=[[1, P]], channel_multiplier=-1)
            pool.affine_select(out=band_mask[:, 1], in_=band_mask[:, 1], compare_op=ALU.is_ge, fill=NEG_INF,
                               base=0, pattern=[[-1, P]], channel_multiplier=1).then_inc(consts_ready, 1)

            def ada_ctx(u):
                for k in range(1, KD):
                    pool.wait_ge(ada_prod_done, u * KD + k + 1)
                    if k == 1:
                        if not isinstance(u, int) or u > 0:
                            pool.wait_ge(ada_turned, u)
                        pool.tensor_tensor(ada_acc[:, 1], ada_tmp[:, 0], ada_tmp[:, 1], ALU.add).then_inc(ada_ctx_done, 2)
                    else:
                        pool.wait_ge(ada_ctx_done, u * KD + k)
                        pool.tensor_tensor(ada_acc[:, 1], ada_acc[:, 1], ada_tmp[:, k % 2], ALU.add).then_inc(ada_ctx_done, 1)

            def sum_squares(n, d, width):
                pool.wait_ge(sq_done, KD * n + d + 1)
                slot = d % 2 if isinstance(d, int) else None
                src = sq[:, slot, 0:width]
                if d == 0:
                    if n > 0:
                        pool.wait_ge(ssq_ready, n)
                    pool.tensor_copy(acc[:, 0:width], src).then_inc(acc_done, 1)
                else:
                    pool.wait_ge(acc_done, KD * n + d)
                    pool.tensor_tensor(acc[:, 0:width], acc[:, 0:width], src, ALU.add).then_inc(acc_done, 1)

            for u in range(UNITS_PER_STAGE):
                ada_ctx(u)
            for d in range(KD):
                sum_squares(0, d, TOK)
            for s in stages:
                layer, n, ow = s["layer"], s["n"], s["out_width"]
                next_w = SEQ if n + 1 == 6 or ow == SEQ else TOK
                if s["kind"] == "mix":
                    pool.wait_ge(x_ready, KD * (n + 1))
                    pool.memset(wf[:], 0.0).then_inc(wf_zeroed, 1)
                    pool.wait_ge(tab_loaded, 48 * (layer + 1))
                    for q in range(8):
                        g, sl, width = 8 * layer + q, q % 2, w_in_width(layer, ROPED[q])
                        pool.wait_ge(rot_done, g + 1)
                        if q >= 2:
                            pool.wait_ge(qlo_done, g - 1)
                        if width == TOK:
                            pool.tensor_copy(roped[:, sl, SEQ:TOK], un[:, sl, SEQ:TOK])
                        pool.tensor_tensor(rot[:, sl], rot[:, sl], rope_tab[:, 1], ALU.mult).then_inc(rope_done, 1)
                        pool.wait_ge(rope_done, 2 * g + 1)
                        pool.tensor_tensor(roped[:, sl, 0:SEQ], rot[:, sl], ucos[:, sl], ALU.add).then_inc(rope_done, 1)
                    for i, (b, kv, q, g) in enumerate(s["tiles"]):
                        si = s["scores"] + i
                        lo = SEQ - P * len(key_blocks(b, q))
                        pool.wait_ge(inv_ready, si + 1)
                        pool.tensor_scalar(prob[:, i % 2, lo:TOK], prob[:, i % 2, lo:TOK], row_inv[:, i % 4:i % 4 + 1], None,
                                           ALU.mult).then_inc(pn_ready, 1)
                    for d in range(KD):
                        sum_squares(n + 1, d, ow)
                    continue
                for g in range(GROUPS):
                    u0 = plan.ada.get((n, g))
                    if g == 0:
                        if u0 is not None:
                            with pool.Fori(0, KD) as i:
                                ada_ctx(u0 + i)
                    else:
                        for d in range(KD):
                            if u0 is not None:
                                ada_ctx(u0 + d)
                            sum_squares(n + 1, d, ow)

        def act_w_in(act, s, split_hi):
            layer, t = s["layer"], s["t"]
            e0, q0 = W_IN_TILES * layer, 8 * layer
            act.preload_act_table(ACT.Sqrt)

            def round_qk(q):
                width = w_in_width(layer, ROPED[q])
                act.wait_ge(rope_done, 2 * (q0 + q) + 2)
                if q0 + q >= 2:
                    act.wait_ge(stored[q % 2], 32 * ((q0 + q) // 2))
                act.activation(qkh[:, q % 2, 0:width], roped[:, q % 2, 0:width], ACT.Copy).then_inc(qhi_done, 1)

            def head_std(j):
                width = w_in_width(layer, j)
                act.wait_ge(bn_done, 4 * layer + j - KB + 1)
                if 4 * layer + j - KB >= 1:
                    act.wait_ge(unorm_done, 4 * layer + j - KB)
                act.activation(rstd[:, 0:width], side[:, 0:width], ACT.Sqrt, bias=eps[:], scale=1.0 / HD).then_inc(bstd_done, 1)

            for j in range(W_IN_TILES):
                tt = t + j
                width = w_in_width(layer, j)
                split_hi(tt + 1, (tt + 1) % 2, NK[tt + 1])
                if j == 2:
                    act.wait_ge(four_mm, layer + 1)
                    act.activation(four[:].rearrange("p c n -> p (c n)"), bank[0][:, 0:4 * P], ACT.Copy).then_inc(four_ready, 1)
                if j in (4, 5):
                    b = j - 4
                    for half, (a, n_) in enumerate(((0, 4), (4, 2))):
                        act.wait_ge(v_turned, 4 * layer + 2 * b + half + 1)
                        for kv, col in ((0, 0), (1, 3 * HD)):
                            last = act.activation(v2[:, b, a:a + n_, col:col + HD],
                                                  bank[half][:, 0:n_ * P].rearrange("p (n f) -> p n f", f=P)[:, :, kv * HD:kv * HD + HD], ACT.Copy)
                        last.then_inc(vhi_done, 1)
                if j == 4:
                    for blk in (0, 2, 4):
                        act.wait_ge(f1_done, 6 * layer + blk + 1)
                        act.activation(v1[:, blk].rearrange("p c n -> p (c n)"), bank[0][:, 0:4 * P], ACT.Copy).then_inc(v1_even, 1)
                if j == 6:
                    for c in range(2):
                        wd = w_in_width(layer, 0)
                        act.wait_ge(f2_done, 2 * layer + c + 1)
                        act.activation(uf[:, c, 0:wd], side[:, 0:wd], ACT.Copy).then_inc(f2_read, 1)
                act.wait_ge(mm_done, tt + 1)
                if j in UF:
                    act.activation(uf[:, j, 0:width], ring[j % 2][:, 0:width], ACT.Copy).then_inc(evac_done, 1)
                else:
                    if j in (4, 5):
                        act.wait_ge(v_turned, 4 * layer + 2 * (j - 4) + 2)
                    if j >= 6:
                        act.wait_ge(rope_done, 2 * (q0 + j - 6) + 2)
                    last = act.activation(un[:, j % 2, 0:width], ring[j % 2][:, 0:width], ACT.Copy)
                    if j < KB:
                        last.then_inc(evac_done, 1)
                    else:
                        if j > KB:
                            head_std(j - 1)
                        act.activation(acc[:, 0:width], ring[j % 2][:, 0:width], ACT.Square).then_inc(evac_done, 1)
                if j - 2 >= 4:
                    round_qk(j - 6)
            head_std(QB[2])
            round_qk(6)
            for c in range(2):
                act.wait_ge(mm_done, t + W_IN_TILES)
                act.activation(xh[:, 6 + c, 0:w_in_width(layer, 0)], uf[:, c, 0:w_in_width(layer, 0)], ACT.Copy).then_inc(fhi_done, 1)
            round_qk(7)

        @block.scalar
        def _(act):
            def split_hi(t, slot, nk):
                if isinstance(t, int):
                    act.wait_ge(w_loaded[slot], 16 * (t // 2 + 1))
                else:
                    act.wait_ge(w_loaded[slot], (t + (2 - slot)) * 8)
                if not isinstance(t, int) or t >= 2:
                    act.wait_ge(mm_done, t - 1)
                act.activation(whi[:, slot, 0:nk * P], raw[:, slot, 0:nk * P], ACT.Copy).then_inc(whi_ready, 1)

            def ada_products(u, buf, loaded, value):
                act.wait_ge(loaded, value)
                for k in range(KD):
                    if not isinstance(u, int) or u * KD + k >= 2:
                        act.wait_ge(ada_ctx_done, u * KD + k - 1)
                    act.activation(ada_tmp[:, k % 2], buf[:, k], ACT.Copy, scale=scond[:, 1, k:k + 1]).then_inc(ada_prod_done, 1)

            def square(n, d, width):
                if d >= 2:
                    act.wait_ge(acc_done, KD * n + d - 1)
                act.activation(sq[:, d % 2, 0:width], h[:, d, 0:width], ACT.Square).then_inc(sq_done, 1)

            def norm(n, width, layer, stage):
                act.preload_act_table(ACT.Sqrt)
                act.wait_ge(ssq_ready, n + 1)
                act.activation(rstd[:, 0:width], side[:, 0:width], ACT.Sqrt, bias=eps[:], scale=1.0 / D_MODEL).then_inc(std_done, 1)
                if layer is None:
                    return
                act.wait_ge(vec_ready, 4 * (n + 1))
                for d in range(KD):
                    act.wait_ge(t1_ready, KD * n + d + 1)
                    if d >= 2:
                        act.wait_ge(x_ready, KD * n + d - 1)
                    for c, (a, b) in enumerate(spans(width)):
                        col = MODC * layer + 3 * KD * stage + d
                        act.activation(t2[:, d % 2, a:b], t1[:, d % 2, a:b], ACT.Identity,
                                       bias=modv[:, c, col:col + 1], scale=vec_scale[:, c, d:d + 1])
                        last = act.activation(xh[:, d, a:b], t1[:, d % 2, a:b], ACT.Identity,
                                              bias=modv[:, c, col:col + 1], scale=vec_scale[:, c, d:d + 1])
                    last.then_inc(mod_done, 1)

            act.preload_act_table(ACT.Silu)
            act.wait_ge(const_loaded, 16 * 7)
            act.wait_ge(consts_ready, CONSTS)
            act.activation(scond[:], cond[:], ACT.Silu).then_inc(cond_ready, 1)
            act.activation(sinks8[:], sinks[:], ACT.Copy, scale=1.0 / SCALE).then_inc(sink_ready, 1)
            act.wait_ge(cond_ready, 1)
            for u in range(UNITS_PER_STAGE):
                ada_products(u, ada_first[u % 4], ada_first_loaded[u % 4], 16 * (u // 4 + 1))
            split_hi(0, 0, NK[0])
            act.wait_ge(h_loaded, 32)
            for d in range(KD):
                square(0, d, TOK)
            norm(0, TOK, 0, 0)

            for s in stages:
                layer, n, width, ow = s["layer"], s["n"], s["width"], s["out_width"]
                t = s["t"]
                if s["kind"] == "mix":
                    act_w_in(act, s, split_hi)
                    tiles = s["tiles"]
                    act.preload_act_table(ACT.Exp)
                    for i in range(len(tiles) + 8):
                        if i < len(tiles):
                            b, kv, q, g = tiles[i]
                            si = s["scores"] + i
                            lo = SEQ - P * len(key_blocks(b, q))
                            act.wait_ge(nm_ready, si + 1)
                            if i >= 2:
                                act.wait_ge(p_turned, si - 1)
                            act.activation(prob[:, i % 2, lo:TOK], ring[(s["r"] + W_IN_TILES + i) % 2][:, lo:TOK], ACT.Exp,
                                           bias=neg_max[:, i % 4:i % 4 + 1], scale=SCALE,
                                           accum_out=row_sum[:, i % 4:i % 4 + 1]).then_inc(exp_done, 1)
                            if b == 0:
                                sc = 6 * layer + 3 * kv + g
                                act.activation(sink_exp[:, i % 4:i % 4 + 1], sinks[:, sc:sc + 1], ACT.Exp,
                                               bias=neg_max[:, i % 4:i % 4 + 1], scale=1.0).then_inc(sink_exp_done, 1)
                        j = i - 2
                        if 0 <= j < len(tiles):
                            b, kv, q, g = tiles[j]
                            sj, tr = s["scores"] + j, (s["scores"] + j) // 3
                            nb = len(key_blocks(b, q)) + 2
                            if j == 0:
                                act.wait_ge(qlo_done, 8 * (layer + 1))
                                act.wait_ge(stored[0], 32 * 4 * (layer + 1))
                                act.wait_ge(stored[1], 32 * 4 * (layer + 1))
                            act.wait_ge(p_turned, sj + 1)
                            if g == 0 and j // 3 >= 2:
                                act.wait_ge(pv_done, tr - 1)
                            act.activation(pth[:, j // 3 % 2, 0:nb, g * P:(g + 1) * P],
                                           side[:, 0:nb * P].rearrange("p (n q) -> p n q", q=P), ACT.Copy).then_inc(pth_done, 1)
                        k = i - 6
                        if k >= 0 and k % 3 == 0 and k // 3 < len(tiles) // 3:
                            b, kv, q, g = tiles[k]
                            tr = s["scores"] // 3 + k // 3
                            here, there = slice(kv * HD, kv * HD + HD), slice((1 - kv) * HD, (1 - kv) * HD + HD)
                            act.wait_ge(pv_done, tr + 1)
                            act.activation(corr[here, k // 3 % 2], bank[k // 3 % 2][there, 0:3 * P], ACT.Copy).then_inc(corr_done, 1)
                        k = i - 7
                        if k >= 0 and k % 3 == 0 and k // 3 < len(tiles) // 3:
                            b, kv, q, g = tiles[k]
                            tr = s["scores"] // 3 + k // 3
                            here = slice(kv * HD, kv * HD + HD)
                            act.wait_ge(osum_done, tr + 1)
                            act.activation(xh[here, 3 * b:3 * b + 3, q * P:(q + 1) * P],
                                           osum[here, k // 3 % 2].rearrange("p (g q) -> p g q", q=P), ACT.Copy).then_inc(ohi_done, 1)
                    for d in range(W_OUT_TILES):
                        tt = t + W_IN_TILES + d + 1
                        split_hi(tt, tt % 2, NK[tt])
                        act.wait_ge(resid_done, s["resid"] + d + 1)
                        square(n + 1, d, ow)
                    norm(n + 1, stages[n + 1]["width"], layer, 2)
                    continue
                act.preload_act_table(ACT.Silu)
                for g in range(GROUPS):
                    p0 = s["pairs"] + g * GF

                    def pair(tt, f, pi, nk_next):
                        split_hi(tt + 1, 1, KD)
                        act.wait_ge(mm_done, tt + 1)
                        if not isinstance(pi, int) or pi > 0:
                            act.wait_ge(prod_done, pi)
                        act.activation(sil[:, 0:width], ring[0][:, 0:width], ACT.Silu).then_inc(silu_done, 1)
                        split_hi(tt + 2, 0, nk_next)
                        act.wait_ge(prod_done, pi + 1)
                        act.activation(ah[:, f, 0:width], atmp[:, 0:width], ACT.Copy).then_inc(ahi_done, 1)

                    pair(t, 0, p0, KD)
                    with act.Fori(1, GF - 1) as i:
                        pair(t + 2 * i, i, p0 + i, KD)
                    pair(t + 2 * GF - 2, GF - 1, p0 + GF - 1, GF)
                    t += 2 * GF
                    u0 = plan.ada.get((n, g))
                    if g == 0:
                        def down(tt, d, slot, nk_next):
                            split_hi(tt + 1, 1 - slot, nk_next)
                            if u0 is not None:
                                ada_products(u0 + d, ada_buf, ada_loaded, (u0 + d - UNITS_PER_STAGE + 1) * 16)
                        with act.Fori(0, KD // 2 - 1) as i:
                            for u in range(2):
                                down(t + u + 2 * i, 2 * i + u, u, GF)
                        down(t + KD - 2, KD - 2, 0, GF)
                        down(t + KD - 1, KD - 1, 1, KD)
                    else:
                        for d in range(KD):
                            if t + d + 1 < N_TILES:
                                split_hi(t + d + 1, (d + 1) % 2, NK[t + d + 1])
                            if u0 is not None:
                                ada_products(u0 + d, ada_buf, ada_loaded, (u0 + d - UNITS_PER_STAGE + 1) * 16)
                            act.wait_ge(resid_done, s["resid"] + KD + d + 1)
                            square(n + 1, d, ow)
                    t += KD
                if n + 1 < len(stages):
                    nx = stages[n + 1]
                    norm(n + 1, nx["width"], nx["layer"], 1 if nx["kind"] == "mix" else 0)
                else:
                    norm(n + 1, SEQ, None, None)

        def dve_w_in(dve, s, split_lo):
            layer, t = s["layer"], s["t"]
            e0, q0 = W_IN_TILES * layer, 8 * layer

            def head_norm_rope(j):
                q, sl, width = j - 4, j % 2, w_in_width(layer, j)
                if j >= KB:
                    b = 4 * layer + j - KB
                    dve.wait_ge(bstd_done, b + 1)
                    dve.reciprocal(rstd[:, 0:width], rstd[:, 0:width]).then_inc(brstd_done, 1)
                    dve.wait_ge(brstd_done, b + 1)
                    kq = 2 * layer + (1 if j == KB else 0)
                    dve.scalar_tensor_tensor(out=un[:, sl, 0:width], in0=un[:, sl, 0:width], scalar=qkg[:, kq:kq + 1],
                                             in1=rstd[:, 0:width], op0=ALU.mult, op1=ALU.mult).then_inc(unorm_done, 1)
                    dve.wait_ge(unorm_done, b + 1)
                dve.wait_ge(evac_done, e0 + j + 1)
                if q == 0:
                    dve.wait_ge(tab_loaded, 48 * (layer + 1))
                dve.stream_shuffle(rot[:, sl], un[:, sl, 0:SEQ], [i ^ 16 for i in range(32)])
                dve.tensor_tensor(ucos[:, sl], un[:, sl, 0:SEQ], rope_tab[:, 0], ALU.mult).then_inc(rot_done, 1)

            def rest_qk(q):
                width = w_in_width(layer, ROPED[q])
                dve.wait_ge(qhi_done, q0 + q + 1)
                dve.tensor_tensor(qkl[:, q % 2, 0:width], roped[:, q % 2, 0:width], qkh[:, q % 2, 0:width].bitcast(F32),
                                  ALU.subtract).then_inc(qlo_done, 1)

            for j in range(W_IN_TILES):
                split_lo(t + j + 1, (t + j + 1) % 2, NK[t + j + 1])
                if j in (4, 5):
                    b = j - 4
                    for half, (a, n_) in enumerate(((0, 4), (4, 2))):
                        dve.wait_ge(vhi_done, 4 * layer + 2 * b + half + 1)
                        for kv, hi, lo in ((0, 0, HD), (1, 3 * HD, 2 * HD)):
                            last = dve.tensor_tensor(
                                v2[:, b, a:a + n_, lo:lo + HD],
                                bank[half][:, 0:n_ * P].rearrange("p (n f) -> p n f", f=P)[:, :, kv * HD:kv * HD + HD],
                                v2[:, b, a:a + n_, hi:hi + HD].bitcast(F32), ALU.subtract)
                        last.then_inc(v_ready, 1)
                if j == 4:
                    for blk in (1, 3, 5):
                        dve.wait_ge(f1_done, 6 * layer + blk + 1)
                        dve.tensor_copy(v1[:, blk].rearrange("p c n -> p (c n)"), bank[1][:, 0:4 * P]).then_inc(v1_odd, 1)
                if j - 1 >= 4:
                    head_norm_rope(j - 1)
                if j - 2 >= 4:
                    rest_qk(j - 6)
            head_norm_rope(11)
            rest_qk(6)
            for c in range(2):
                wd = w_in_width(layer, 0)
                dve.wait_ge(fhi_done, 2 * layer + c + 1)
                dve.tensor_tensor(xl[:, 6 + c, 0:wd], uf[:, c, 0:wd], xh[:, 6 + c, 0:wd].bitcast(F32), ALU.subtract).then_inc(mix_ready, 1)
            rest_qk(7)

        def dve_attention(dve, s):
            layer, tiles = s["layer"], s["tiles"]
            sinks_before = len(tiles) // 2 and sum(len(score_tiles(l)) // 2 for l in range(layer))
            for i in range(len(tiles) + 8):
                if i < len(tiles):
                    b, kv, q, g = tiles[i]
                    si = s["scores"] + i
                    lo = SEQ - P * len(key_blocks(b, q))
                    dve.wait_ge(sc_done, si + 1)
                    dve.reduce_max(row_max[:, i % 2:i % 2 + 1], ring[(s["r"] + W_IN_TILES + i) % 2][:, lo:TOK], AX.X).then_inc(max_done, 1)
                    dve.wait_ge(max_done, si + 1)
                    m, nm = row_max[:, i % 2:i % 2 + 1], neg_max[:, i % 4:i % 4 + 1]
                    if b == 0:
                        if i == 0:
                            dve.wait_ge(sink_ready, 1)
                        sc = 6 * layer + 3 * kv + g
                        dve.tensor_scalar(nm, m, sinks8[:, sc:sc + 1], -SCALE, ALU.max, ALU.mult).then_inc(nm_ready, 1)
                    else:
                        dve.tensor_scalar(nm, m, -SCALE, None, ALU.mult).then_inc(nm_ready, 1)
                j = i - 1
                if 0 <= j < len(tiles):
                    b, kv, q, g = tiles[j]
                    sj = s["scores"] + j
                    tot = row_sum[:, j % 4:j % 4 + 1]
                    dve.wait_ge(exp_done, sj + 1)
                    if b == 0:
                        dve.wait_ge(sink_exp_done, sinks_before + j + 1)
                        dve.tensor_tensor(row_tot[:, j % 2:j % 2 + 1], tot, sink_exp[:, j % 4:j % 4 + 1], ALU.add).then_inc(tot_done, 1)
                        dve.wait_ge(tot_done, sinks_before + j + 1)
                        tot = row_tot[:, j % 2:j % 2 + 1]
                    dve.reciprocal(row_inv[:, j % 4:j % 4 + 1], tot).then_inc(inv_ready, 1)
                j = i - 2
                if 0 <= j < len(tiles):
                    b, kv, q, g = tiles[j]
                    sj = s["scores"] + j
                    nb = len(key_blocks(b, q)) + 2
                    if j == 0:
                        dve.wait_ge(stored[0], 32 * 4 * (layer + 1))
                        dve.wait_ge(stored[1], 32 * 4 * (layer + 1))
                    dve.wait_ge(pth_done, sj + 1)
                    part = slice(g * P, (g + 1) * P)
                    dve.tensor_tensor(ptl[:, j // 3 % 2, 0:nb, part], side[:, 0:nb * P].rearrange("p (n q) -> p n q", q=P),
                                      pth[:, j // 3 % 2, 0:nb, part].bitcast(F32), ALU.subtract).then_inc(pt_ready, 1)
                k = i - 6
                if k >= 0 and k % 3 == 0 and k // 3 < len(tiles) // 3:
                    b, kv, q, g = tiles[k]
                    tr = s["scores"] // 3 + k // 3
                    here = slice(kv * HD, kv * HD + HD)
                    dve.wait_ge(corr_done, tr + 1)
                    dve.tensor_tensor(osum[here, k // 3 % 2], bank[k // 3 % 2][here, 0:3 * P], corr[here, k // 3 % 2],
                                      ALU.add).then_inc(osum_done, 1)
                k = i - 7
                if k >= 0 and k % 3 == 0 and k // 3 < len(tiles) // 3:
                    b, kv, q, g = tiles[k]
                    tr = s["scores"] // 3 + k // 3
                    here, cols = slice(kv * HD, kv * HD + HD), slice(q * P, (q + 1) * P)
                    dve.wait_ge(ohi_done, tr + 1)
                    dve.tensor_tensor(xl[here, 3 * b:3 * b + 3, cols], osum[here, k // 3 % 2].rearrange("p (g q) -> p g q", q=P),
                                      xh[here, 3 * b:3 * b + 3, cols].bitcast(F32), ALU.subtract).then_inc(mix_ready, 1)

        @block.vector
        def _(dve):
            def split_lo(t, slot, nk):
                dve.wait_ge(whi_ready, t + 1)
                dve.tensor_tensor(wlo[:, slot, 0:nk * P], raw[:, slot, 0:nk * P], whi[:, slot, 0:nk * P].bitcast(F32),
                                  ALU.subtract).then_inc(wlo_ready, 1)

            def ada_lat(u, buf, loaded, value):
                dve.wait_ge(loaded, value)
                for k in range(KD):
                    if k == 0:
                        if not isinstance(u, int) or u > 0:
                            dve.wait_ge(ada_turned, u)
                        dve.tensor_scalar(ada_acc[:, 0], buf[:, 0], scond[:, 0, 0:1], None, ALU.mult).then_inc(ada_lat_done, 1)
                    else:
                        dve.wait_ge(ada_lat_done, u * KD + k)
                        dve.scalar_tensor_tensor(out=ada_acc[:, 0], in0=buf[:, k], scalar=scond[:, 0, k:k + 1],
                                                 in1=ada_acc[:, 0], op0=ALU.mult, op1=ALU.add).then_inc(ada_lat_done, 1)

            def ada_reduce(u):
                dve.wait_ge(ada_turned, u + 1)
                for c in range(2):
                    dve.tensor_reduce(ada_sum[:, c], bank[c][:, 0:ADA_COLS].rearrange("p (n k) -> p n k", k=P), AX.X,
                                      ALU.add).then_inc(ada_red_done, 1)
                dve.wait_ge(ada_red_done, u * 4 + 2)
                for c in range(2):
                    dve.tensor_tensor(modv[:, c, bass.ds(u * UC, UC)], ada_sum[:, c], bias_ada[:, bass.ds(u * UC, UC)],
                                      ALU.add).then_inc(ada_red_done, 1)

            def norm(n, width, layer, stage, units, gate_scale):
                if layer is not None:
                    dve.wait_ge(ada_red_done, 4 * units)
                    if n > 0:
                        dve.wait_ge(resid_done, stages[n]["resid"])
                    col = MODC * layer + 3 * KD * stage
                    for c in range(2):
                        dve.scalar_tensor_tensor(out=vec_scale[:, c], in0=modv[:, c, col + KD:col + 2 * KD], scalar=1.0,
                                                 in1=gain[:, 3 * layer + stage], op0=ALU.add, op1=ALU.mult).then_inc(vec_ready, 1)
                        dve.tensor_scalar(vec_gate[:, c], modv[:, c, col + 2 * KD:col + 3 * KD], gate_scale, None,
                                          ALU.mult).then_inc(vec_ready, 1)
                dve.wait_ge(std_done, n + 1)
                dve.reciprocal(rstd[:, 0:width], rstd[:, 0:width]).then_inc(rstd_ready, 1)
                dve.wait_ge(rstd_ready, n + 1)
                if layer is None:
                    for d in range(KD):
                        dve.scalar_tensor_tensor(out=h[:, d, 0:SEQ], in0=h[:, d, 0:SEQ], scalar=gain_final[:, d:d + 1],
                                                 in1=rstd[:, 0:SEQ], op0=ALU.mult, op1=ALU.mult).then_inc(out_ready, 1)
                    return
                for d in range(KD + 1):
                    if d < KD:
                        if d >= 2:
                            dve.wait_ge(mod_done, KD * n + d - 1)
                        dve.tensor_tensor(t1[:, d % 2, 0:width], h[:, d, 0:width], rstd[:, 0:width], ALU.mult).then_inc(t1_ready, 1)
                    if d >= 1:
                        dve.wait_ge(mod_done, KD * n + d)
                        dve.tensor_tensor(xl[:, d - 1, 0:width], t2[:, (d - 1) % 2, 0:width], xh[:, d - 1, 0:width].bitcast(F32),
                                          ALU.subtract).then_inc(x_ready, 1)

            def residual(t_done, d, slot, width):
                dve.wait_ge(mm_done, t_done)
                for c, (a, b) in enumerate(spans(width)):
                    last = dve.scalar_tensor_tensor(out=h[:, d, a:b], in0=ring[slot][:, a:b], scalar=vec_gate[:, c, d:d + 1],
                                                    in1=h[:, d, a:b], op0=ALU.mult, op1=ALU.add)
                last.then_inc(resid_done, 1)

            dve.wait_ge(const_loaded, 16 * 7)
            dve.wait_ge(cond_ready, 1)
            for u in range(UNITS_PER_STAGE):
                ada_lat(u, ada_first[u % 4], ada_first_loaded[u % 4], 16 * (u // 4 + 1))
                ada_reduce(u)
            split_lo(0, 0, NK[0])
            norm(0, TOK, 0, 0, UNITS_PER_STAGE, 0.5)

            for s in stages:
                layer, n, width, ow = s["layer"], s["n"], s["width"], s["out_width"]
                t = s["t"]
                if s["kind"] == "mix":
                    dve_w_in(dve, s, split_lo)
                    dve_attention(dve, s)
                    for d in range(W_OUT_TILES):
                        tt = t + W_IN_TILES + d
                        split_lo(tt + 1, (tt + 1) % 2, NK[tt + 1])
                        residual(tt + 1, d, (s["r"] + W_IN_TILES + len(s["tiles"]) + d) % 2, ow)
                    norm(n + 1, stages[n + 1]["width"], layer, 2, ADA_UNITS * (layer + 1), 0.5)
                    continue
                for g in range(GROUPS):
                    p0 = s["pairs"] + g * GF

                    def pair(tt, f, pi, nk_next):
                        split_lo(tt + 1, 1, KD)
                        split_lo(tt + 2, 0, nk_next)
                        dve.wait_ge(silu_done, pi + 1)
                        dve.wait_ge(mm_done, tt + 2)
                        dve.tensor_tensor(atmp[:, 0:width], sil[:, 0:width], ring[1][:, 0:width], ALU.mult).then_inc(prod_done, 1)
                        dve.wait_ge(ahi_done, pi + 1)
                        dve.tensor_tensor(al[:, f, 0:width], atmp[:, 0:width], ah[:, f, 0:width].bitcast(F32),
                                          ALU.subtract).then_inc(alo_done, 1)

                    pair(t, 0, p0, KD)
                    with dve.Fori(1, GF - 1) as i:
                        pair(t + 2 * i, i, p0 + i, KD)
                    pair(t + 2 * GF - 2, GF - 1, p0 + GF - 1, GF)
                    t += 2 * GF
                    u0 = plan.ada.get((n, g))

                    def down(tt, d, slot, nk_next):
                        if nk_next:
                            split_lo(tt + 1, 1 - slot, nk_next)
                        if u0 is not None:
                            ada_lat(u0 + d, ada_buf, ada_loaded, (u0 + d - UNITS_PER_STAGE + 1) * 16)
                        residual(tt + 1, d, slot, width)
                        if u0 is not None:
                            ada_reduce(u0 + d)

                    for d in range(KD):
                        nt = t + d + 1
                        down(t + d, d, d % 2, NK[nt] if nt < N_TILES else None)
                    t += KD
                if n + 1 < len(stages):
                    nx = stages[n + 1]
                    stage = 1 if nx["kind"] == "mix" else 0
                    units = ADA_UNITS * nx["layer"] + UNITS_PER_STAGE * (stage + 1)
                    norm(n + 1, nx["width"], nx["layer"], stage, units, 1.0 if stage == 1 else 0.5)
                else:
                    norm(n + 1, SEQ, None, None, 0, 1.0)

        def pe_mixer(pe, s, product):
            layer, n, t, r, tiles = s["layer"], s["n"], s["t"], s["r"], s["tiles"]
            x_w = w_in_width(layer, 0)
            blocks = 6 if x_w == TOK else 4
            e0 = W_IN_TILES * layer

            def head_squares(j):
                b, width = 4 * layer + j - KB, w_in_width(layer, j)
                pe.wait_ge(evac_done, e0 + j + 1)
                if j > KB:
                    pe.wait_ge(bstd_done, b)
                for a, c in spans(width):
                    last = pe.matmul(side[:, a:c], head_ones[:], acc[:, a:c], start=True, stop=True)
                last.then_inc(bn_done, 1)

            def turn_values(b):
                pe.wait_ge(evac_done, e0 + 3 + b)
                for half, (a, n_) in enumerate(((0, 4), (4, 2))):
                    if b == 1:
                        pe.wait_ge(v1_even if half == 0 else v1_odd, 3 * layer + 3)
                    elif half == 0:
                        pe.wait_ge(four_ready, layer + 1)
                    for m in range(n_):
                        last = pe.transpose(bank[half][:, m * P:(m + 1) * P], un[:, b, (a + m) * P:(a + m + 1) * P], ident[:])
                    last.then_inc(v_turned, 1)

            for j in range(W_IN_TILES):
                slot_free(pe, r + j)
                pe.wait_ge(wlo_ready, t + j + 1)
                product(ring[j % 2], j % 2, KD, xh, xl, w_in_width(layer, j),
                        k_wait=(lambda k: pe.wait_ge(x_ready, KD * n + k + 1)) if j == 0 else None)
                if j == 1:
                    pe.wait_ge(wf_loaded, 64 * (layer + 1))
                    pe.wait_ge(const_loaded, 16 * 7)
                    for c in range(2):
                        for part in range(2):
                            o = (2 * c + part) * P
                            last = pe.matmul(bank[0][:, o:o + P], chan[:, part], wf[:, c], start=True, stop=True)
                    last.then_inc(four_mm, 1)
                if j == 3:
                    turn_values(0)
                    for blk in range(6):
                        if blk < 2:
                            pe.wait_ge(v_ready, 4 * layer + blk + 1)
                        elif blk % 2 == 0:
                            pe.wait_ge(v1_even, 3 * layer + blk // 2)
                        else:
                            pe.wait_ge(v1_odd, 3 * layer + blk // 2)
                        src = blk if blk < blocks else 0
                        for c in range(2):
                            last = pe.matmul(bank[blk % 2][:, c * 2 * P:(c + 1) * 2 * P], uf[:, c, src * P:(src + 1) * P], four[:, c],
                                             start=True, stop=True)
                        last.then_inc(f1_done, 1)
                if j == 4:
                    turn_values(1)
                if j == 5:
                    pe.wait_ge(v1_even, 3 * layer + 3)
                    pe.wait_ge(v1_odd, 3 * layer + 3)
                    pe.wait_ge(tab_loaded, 48 * (layer + 1))
                    for c in range(2):
                        if c == 1:
                            pe.wait_ge(f2_read, 2 * layer + 1)
                        for tab, b0, nb, (lo, hi) in ((pos_lat, 0, 4, (0, SEQ)), (pos_ctx, 4, 2, (SEQ, TOK)))[:2 if blocks == 6 else 1]:
                            for m in range(nb):
                                for part in range(2):
                                    last = pe.matmul(side[:, lo:hi], v1[:, b0 + m, c, part * P:(part + 1) * P], tab[:, part, m],
                                                     start=(m == 0 and part == 0), stop=(m == nb - 1 and part == 1))
                        last.then_inc(f2_done, 1)
                if j > KB:
                    if j == KB + 1:
                        pe.wait_ge(f2_read, 2 * layer + 2)
                    head_squares(j - 1)
            head_squares(QB[2])
            t += W_IN_TILES
            r += W_IN_TILES

            def scores(i):
                b, kv, q, g = tiles[i]
                keys = key_blocks(b, q)
                lo = SEQ - P * len(keys)
                z = i // (len(tiles) // 4)
                out = ring[(r + i) % 2]
                slot_free(pe, r + i)
                if i % (len(tiles) // 4) == 0:
                    pe.wait_ge(stack_loaded[z % 2], 64 * (2 * layer + z // 2 + 1))
                query = q2[:, z % 2, g, q * P:(q + 1) * P]
                if keys:
                    k0 = keys[0] * P
                    edges = []
                    if b == 0:
                        if keys[0] == q - 1:
                            edges.append((0, lo))
                        if keys[-1] == q + 1:
                            edges.append((1, SEQ - P))
                    for part in range(2):
                        pe.matmul(out[:, lo:SEQ], query, k2[:, z % 2, part, k0:k0 + SEQ - lo], start=(part == 0),
                                  stop=(part == 1 and not edges))
                    for m, (e, col) in enumerate(edges):
                        pe.matmul(out[:, col:col + P], ident_b[:], band_mask[:, e], start=False, stop=(m == len(edges) - 1))
                for part in range(2):
                    last = pe.matmul(out[:, SEQ:TOK], query, k2[:, z % 2, part, SEQ:TOK], start=(part == 0), stop=(part == 1))
                last.then_inc(sc_done, 1)

            def turn_probs(i):
                b, kv, q, g = tiles[i]
                si = s["scores"] + i
                nb = len(key_blocks(b, q)) + 2
                lo = TOK - nb * P
                pe.wait_ge(pn_ready, si + 1)
                if i >= 1:
                    pe.wait_ge(pt_ready, si)
                else:
                    pe.wait_ge(bstd_done, 4 * (layer + 1))
                for m in range(nb):
                    last = pe.transpose(side[:, m * P:(m + 1) * P], prob[:, i % 2, lo + m * P:lo + (m + 1) * P], ident[:])
                last.then_inc(p_turned, 1)

            def weigh_values(k):
                b, kv, q, g = tiles[3 * k]
                tr = s["scores"] // 3 + k
                keys = key_blocks(b, q) + [4, 5]
                pe.wait_ge(pt_ready, s["scores"] + 3 * k + 3)
                pe.wait_ge(v_ready, 4 * (layer + 1))
                if k >= 2:
                    pe.wait_ge(osum_done, tr - 1)
                for m, kb in enumerate(keys):
                    for pt in (pth, ptl):
                        last = pe.matmul(bank[k % 2][:, 0:3 * P], v2[:, b, kb, kv * P:(kv + 1) * P], pt[:, k % 2, m, :],
                                         start=(m == 0 and pt is pth), stop=(m == len(keys) - 1 and pt is ptl))
                last.then_inc(pv_done, 1)

            for i in range(len(tiles) + 6):
                if i < len(tiles):
                    scores(i)
                if 0 <= i - 2 < len(tiles):
                    turn_probs(i - 2)
                k = i - 5
                if k >= 0 and k % 3 == 0 and k // 3 < len(tiles) // 3:
                    weigh_values(k // 3)
            r += len(tiles)
            ready = dict(zip((6, 0, 3), mix_counts(layer)))
            for d in range(W_OUT_TILES):
                slot_free(pe, r + d)
                pe.wait_ge(wlo_ready, t + d + 1)
                product(ring[(r + d) % 2], d % 2, KD, xh, xl, s["out_width"], order=[6, 7, 0, 1, 2, 3, 4, 5],
                        k_wait=(lambda k: pe.wait_ge(mix_ready, ready[k]) if k in ready else None) if d == 0 else None)

        @block.tensor
        def _(pe):
            def product(out, slot, nk, xs_hi, xs_lo, width, done=None, k_wait=None, order=None):
                order = order or list(range(nk))
                for i, k in enumerate(order):
                    if k_wait:
                        k_wait(k)
                    w_h, w_l = whi[:, slot, k * P:(k + 1) * P], wlo[:, slot, k * P:(k + 1) * P]
                    for m, (w, x) in enumerate(((w_h, xs_hi), (w_h, xs_lo), (w_l, xs_hi))):
                        for a, b in spans(width):
                            last = pe.matmul(out[:, a:b], w, x[:, k, a:b], start=(i == 0 and m == 0),
                                             stop=(i == nk - 1 and m == 2))
                last.then_inc(mm_done, 1)

            def sum_chunks(n, width):
                pe.wait_ge(acc_done, KD * (n + 1))
                for a, b in spans(width):
                    last = pe.matmul(side[:, a:b], ones[:], acc[:, a:b], start=True, stop=True)
                last.then_inc(ssq_ready, 1)

            def ada_turn(u):
                pe.wait_ge(ada_lat_done, (u + 1) * KD)
                pe.wait_ge(ada_ctx_done, (u + 1) * KD)
                if not isinstance(u, int) or u > 0:
                    pe.wait_ge(ada_red_done, u * 4)
                for c in range(2):
                    for m in range(UC):
                        last = pe.transpose(bank[c][:, m * P:(m + 1) * P], ada_acc[:, c, m * P:(m + 1) * P], ident[:])
                last.then_inc(ada_turned, 1)

            pe.wait_ge(consts_ready, CONSTS)
            for u in range(UNITS_PER_STAGE):
                ada_turn(u)
            sum_chunks(0, TOK)

            for s in stages:
                layer, n, width, ow = s["layer"], s["n"], s["width"], s["out_width"]
                t, r = s["t"], s["r"]
                if s["kind"] == "mix":
                    pe_mixer(pe, s, product)
                    sum_chunks(n + 1, ow)
                    continue

                def one(tt, slot, first):
                    pe.wait_ge(wlo_ready, tt + 1)
                    product(ring[slot], slot, KD, xh, xl, width,
                            k_wait=(lambda k: pe.wait_ge(x_ready, KD * n + k + 1)) if first else None)

                for g in range(GROUPS):
                    slot_free(pe, r)
                    one(t, 0, g == 0)
                    slot_free(pe, r + 1)
                    one(t + 1, 1, False)
                    with pe.Fori(1, GF) as i:
                        for u in range(2):
                            slot_free(pe, r + u + 2, i, 1)
                            one(t + u + 2 * i, u, False)
                    t += 2 * GF
                    r += 2 * GF
                    a0 = s["pairs"] + g * GF
                    u0 = plan.ada.get((n, g))

                    def down(tt, d, slot):
                        pe.wait_ge(wlo_ready, tt + 1)
                        product(ring[slot], slot, GF, ah, al, width, k_wait=lambda k: pe.wait_ge(alo_done, a0 + k + 1) if k >= GF - 3 else None)
                        if u0 is not None:
                            ada_turn(u0 + d)
                    pe.wait_ge(alo_done, a0 + GF - 3)
                    for u in range(2):
                        slot_free(pe, r + u)
                        down(t + u, u, u)
                    with pe.Fori(1, KD // 2) as i:
                        for u in range(2):
                            slot_free(pe, r + u + 2, i, 1)
                            down(t + u + 2 * i, 2 * i + u, u)
                    t += KD
                    r += KD
                sum_chunks(n + 1, ow)

def columns_of_w_in():
    a_q, a_k, a_v, b_q, b_k, b_v, u = 0, 384, 512, 640, 1024, 1152, 1280
    head = lambda base, i: list(range(base + i * HD, base + (i + 1) * HD))
    run = lambda base: list(range(base, base + P))
    tiles = [run(u), run(u + P), run(a_v), run(b_v), run(a_k)] + [head(a_q, g) + head(a_q, g + 3) for g in range(3)]
    tiles += [run(b_k)] + [head(b_q, g) + head(b_q, g + 3) for g in range(3)]
    return [i for tile in tiles for i in tile]


def rows_of_w_out():
    head = lambda base, i: list(range(base + i * HD, base + (i + 1) * HD))
    rows = [i for base in (0, 384) for g in range(3) for i in head(base, g) + head(base, g + 3)]
    return rows + list(range(768, 1024))


def shape_constants():
    half = HD // 2
    inv = (ROPE_THETA ** (-np.arange(0, half, 2, dtype=np.float32) / half)).astype(np.float32)
    pos = np.arange(SEQ)
    p = np.arange(P) % HD
    place = np.where((p < half)[:, None], (pos // GRID_W)[None], (pos % GRID_W)[None]).astype(np.float32)
    angle = (place * inv[p % 16][:, None]).astype(np.float32).astype(np.float64)
    sign = np.where(p % half < 16, -1.0, 1.0)[:, None]
    rope = np.stack([np.cos(angle), np.sin(angle) * sign], 1).astype(np.float32)

    def dft(n):
        k = np.outer(np.arange(n), np.arange(n)) % n
        return np.cos(2 * np.pi * k / n) / np.sqrt(n), np.sin(2 * np.pi * k / n) / np.sqrt(n)

    cos, sin = dft(HD)
    chan = np.zeros((P, 2, P))
    for g in range(2):
        chan[g * HD:(g + 1) * HD, 0, g * HD:(g + 1) * HD] = cos
        chan[g * HD:(g + 1) * HD, 1, g * HD:(g + 1) * HD] = sin

    def positions(n):
        cos, sin = dft(n)
        return np.stack([cos, -sin]).reshape(2, n // P, P, n).transpose(2, 0, 1, 3)

    f = lambda a: np.ascontiguousarray(a, dtype=np.float32)
    return f(rope), f(chan), f(positions(SEQ)), f(positions(CTX))


def kernel(**inputs):
    import concourse.bacc as bacc
    from concourse.bass_utils import run_bass_kernel_spmd

    a = {k: np.ascontiguousarray(v) for k, v in inputs.items()}
    c = np.ascontiguousarray
    by_feature = lambda v: c(v.reshape(-1, P).T)
    tiles = lambda w, nt: c(w.reshape(DEPTH, -1, P, nt, P).transpose(0, 3, 2, 1, 4).reshape(DEPTH, nt, P, -1))
    gate_up = np.stack([np.stack([tiles(a[f"w{i}_gate"], NF), tiles(a[f"w{i}_up"], NF)], 2) for i in (1, 2)], 1)
    down = np.stack([a[f"w{i}_down"].reshape(DEPTH, GROUPS, GF, P, KD, P).transpose(0, 1, 4, 3, 2, 5) for i in (1, 2)], 1)
    rope, chan, lat, ctx = shape_constants()
    arrays = {
        "x_t": c(a["x"][0].reshape(SEQ, KD, P).transpose(2, 1, 0)),
        "ctx_t": c(a["ctx"][0].reshape(CTX, KD, P).transpose(2, 1, 0)),
        "c_cols": c(np.stack([by_feature(a["c"][0]), by_feature(a["c_ctx"])], 1)),
        "w_ada": c(a["w_ada"].reshape(DEPTH, KD, P, ADA_UNITS, ADA_COLS).transpose(0, 3, 2, 1, 4).reshape(DEPTH * ADA_UNITS, P, KD, ADA_COLS)),
        "b_ada": by_feature(a["b_ada"]),
        "gains": c(np.stack([a["g_ffn1"], a["g_mix"], a["g_ffn2"]], 1).reshape(DEPTH * 3, KD, P).transpose(2, 0, 1)),
        "g_final": by_feature(a["g_final"]),
        "qk_gain": c(np.tile(np.stack([a["g_qn"], a["g_kn"]], 1).reshape(DEPTH * 2, HD), (1, 2)).T),
        "sink": c(np.broadcast_to(a["sink"].reshape(1, -1), (P, DEPTH * 6))),
        "w_in": tiles(a["w_in"][:, :, columns_of_w_in()], W_IN_TILES),
        "w_four": a["w_four"],
        "w_out": tiles(a["w_out"][:, rows_of_w_out(), :], W_OUT_TILES),
        "w_gu": c(gate_up.reshape(2 * DEPTH, NF, 2, P, KD * P)),
        "w_down": c(down.reshape(2 * DEPTH, GROUPS, KD, P, GF * P)),
        "rope": rope, "dft_chan": chan, "dft_lat": lat, "dft_ctx": ctx,
    }
    nc = bacc.Bacc("TRN2", target_bir_lowering=False, num_devices=1)
    args = {k: nc.dram_tensor(k, v.shape, mybir.dt.from_np(v.dtype), kind="ExternalInput").ap() for k, v in arrays.items()}
    out = nc.dram_tensor("out", (P, KD, SEQ), F32, kind="ExternalOutput").ap()
    build(nc, out=out, **args)
    result = run_bass_kernel_spmd(nc, [arrays], core_ids=[0]).results[0]["out"]
    return c(result.transpose(2, 1, 0).reshape(1, SEQ, D_MODEL))
```

```python
from contextlib import ExitStack

import numpy as np
import concourse.bass as bass
from concourse import mybir

F32 = mybir.dt.float32
F32R = mybir.dt.float32r
BF16 = mybir.dt.bfloat16
ALU = mybir.AluOpType
ACT = mybir.ActivationFunctionType
AX = mybir.AxisListType

P = 128
D_MODEL, SEQ, CTX, DEPTH, D_FF = 1024, 512, 256, 2, 2816
GRID_W, HD, N_MOD = 64, 64, 9
NORM_EPS, NEG_INF, ROPE_THETA = 1e-6, -1e30, 10000.0
TOK = SEQ + CTX
KD = D_MODEL // P
NF = D_FF // P
GROUPS = 2
GF = NF // GROUPS
W_IN_TILES, W_OUT_TILES = 12, 8
FFN_TILES = 2 * NF + GROUPS * KD
SCALE = float(HD) ** -0.5
ADA_COLS = 384
ADA_UNITS = N_MOD * D_MODEL // ADA_COLS
UNITS_PER_STAGE = ADA_UNITS // 3
FIRST_UNITS = 6
UC = ADA_COLS // P
MODC = N_MOD * KD

KB, QB, KA, QA, VA, VB, UF = 0, (1, 2, 3), 4, (5, 6, 7), 8, 9, (10, 11)
ROPED = 8
P_RING, LAG = 3, 2


def w_in_width(layer, j):
    return TOK if layer < DEPTH - 1 or j in (VA, VB, KA, KB) else SEQ


def spans(width):
    return [(0, SEQ), (SEQ, TOK)] if width == TOK else [(0, SEQ)]


class Plan:

    def __init__(self):
        self.stages = []
        t = r = resid = 0
        self.release = []
        pairs = scores = 0
        for layer in range(DEPTH):
            last = layer == DEPTH - 1
            for kind in ("ffn1", "mix", "ffn2"):
                width = SEQ if last and kind == "ffn2" else TOK
                s = dict(kind=kind, layer=layer, n=len(self.stages), t=t, r=r, resid=resid, pairs=pairs,
                         width=width, out_width=width if kind != "mix" or not last else SEQ, scores=scores)
                self.stages.append(s)
                if kind == "mix":
                    for j in range(W_IN_TILES):
                        self.release.append(("evac_done", W_IN_TILES * layer + j + 1))
                    s["tiles"] = score_tiles(layer)
                    for i in range(len(s["tiles"])):
                        self.release.append(("exp_done", scores + i + 1))
                    scores += len(s["tiles"])
                    for d in range(KD):
                        self.release.append(("resid_done", resid + d + 1))
                    resid += KD
                    t += W_IN_TILES + W_OUT_TILES
                    r += W_IN_TILES + len(s["tiles"]) + W_OUT_TILES
                else:
                    for g in range(GROUPS):
                        for f in range(GF):
                            self.release.append(("silu_done", pairs + 1))
                            self.release.append(("prod_done", pairs + 1))
                            pairs += 1
                        for d in range(KD):
                            self.release.append(("resid_done", resid + 1))
                            resid += 1
                    t += FFN_TILES
                    r += FFN_TILES
        self.ada, u = {}, 0
        total = DEPTH * ADA_UNITS - FIRST_UNITS
        for key in ((0, 0), (0, 1), (2, 0), (2, 1), (3, 0)):
            self.ada[key] = (u, min(GF - 2, total - u))
            u += self.ada[key][1]
        assert u == total


def score_tiles(layer):
    blocks = 6 if layer < DEPTH - 1 else 4
    return [(b, kv, q, g) for b in range(2) for kv in range(2) for q in range(blocks) for g in range(3)]


def key_blocks(branch, q):
    if q >= 4:
        return []
    return list(range(max(0, q - 1), min(3, q + 1) + 1)) if branch == 0 else [0, 1, 2, 3]


def build(nc, x_t, ctx_t, c_cols, w_ada, b_ada, gains, g_final, qk_gain, sink, w_in, w_four, w_out,
          w_gu, w_down, rope, dft_chan, dft_lat, dft_ctx, out):
    plan = Plan()
    stages = plan.stages
    ctx = ExitStack()
    with ctx:
        sem_of = {}

        def sem(name):
            sem_of[name] = ctx.enter_context(nc.semaphore(name))
            return sem_of[name]

        at = [nc.sbuf_base + 31 & ~31]

        def sb(name, shape, dt=F32, offset=None):
            size = int(np.prod(shape[1:])) * (2 if dt == BF16 else 4)
            if offset is None:
                offset = at[0]
                at[0] += size + 31 & ~31
            return nc.alloc_sbuf_tensor_at(name, shape, dt, offset=offset)

        h = sb("h", [P, KD, TOK])
        xh = sb("xh", [P, KD, TOK], F32R)
        xl = sb("xl", [P, KD, TOK], F32R)
        raw = sb("raw", [P, 2, GF * P])
        whi = sb("whi", [P, 2, GF * P], F32R)
        wlo = sb("wlo", [P, 2, GF * P], F32R)
        ones = sb("ones", [P, P])
        head_ones = sb("head_ones", [P, P])
        ident = sb("ident", [P, P])
        ident_b = sb("ident_b", [P, P], BF16)
        band_mask = sb("band_mask", [P, 2, P], BF16)
        chan = sb("chan", [P, 2, P])
        modv = sb("modv", [P, 2, DEPTH * MODC])
        bias_ada = sb("bias_ada", [P, DEPTH * MODC])
        gain = sb("gain", [P, DEPTH * 3, KD])
        gain_final = sb("gain_final", [P, KD])
        qkg = sb("qkg", [P, DEPTH * 2])
        sinks = sb("sinks", [P, DEPTH * 6])
        sinks8 = sb("sinks8", [P, DEPTH * 6])
        cond = sb("cond", [P, 2, KD])
        scond = sb("scond", [P, 2, KD])
        eps = sb("eps", [P, 1])
        ada_sum = sb("ada_sum", [P, 2, UC])
        vec_scale = sb("vec_scale", [P, 2, KD])
        vec_gate = sb("vec_gate", [P, 2, KD])
        row_max = sb("row_max", [P, 2])
        neg_max = sb("neg_max", [P, 4])
        row_sum = sb("row_sum", [P, 4])
        sink_exp = sb("sink_exp", [P, 4])
        row_tot = sb("row_tot", [P, 2])
        row_inv = sb("row_inv", [P, 8])
        acc = sb("acc", [P, TOK])
        rstd = sb("rstd", [P, TOK])
        work = at[0]
        room = nc.sbuf_usable_end - work

        ah = sb("ah", [P, GF, TOK], F32R, work)
        al = sb("al", [P, GF, TOK], F32R, work + 33792)
        sil = sb("sil", [P, TOK], F32, work + 67584)
        atmp = sb("atmp", [P, TOK], F32, work + 70656)
        sq = sb("sq", [P, 2, TOK], F32, work + 67584)
        ada_buf = sb("ada_buf", [P, KD, ADA_COLS], F32, work + 73728)
        ada_acc = sb("ada_acc", [P, 2, ADA_COLS], F32, work + 86016)
        ada_tmp = sb("ada_tmp", [P, 2, ADA_COLS], F32, work + 89088)
        assert room >= 92160, room
        ada_first = [sb(f"ada_first{i}", [P, KD, ADA_COLS], F32, work + 12288 * i) for i in range(4)]
        ada_rows = sb("ada_rows", [2, 2, ADA_COLS], F32, work + 86016)
        t1 = sb("t1", [P, 4, TOK], F32, work + 49152)
        v2 = sb("v2", [P, 2, 6, 2 * P], F32R, work)
        qkh = sb("qkh", [P, 2, TOK], F32R, work + 12288)
        qkl = sb("qkl", [P, 2, TOK], F32R, work + 18432)
        roped = sb("roped", [P, 2, TOK], F32, work + 24576)
        rot = sb("rot", [P, 2, SEQ], F32, work + 30720)
        ucos = sb("ucos", [P, 2, SEQ], F32, work + 34816)
        rope_tab = sb("rope_tab", [P, 2, SEQ], F32, work + 38912)
        un = sb("un", [P, 2, TOK], F32, work + 43008)
        uf = sb("uf", [P, 2, TOK], F32, work + 49152)
        pos_lat = sb("pos_lat", [P, 2, 4, SEQ], F32, work + 55296)
        pos_ctx = sb("pos_ctx", [P, 2, 2, CTX], F32, work + 71680)
        v1 = sb("v1", [P, 6, 2, 2 * P], F32, work + 75776)
        four = sb("four", [P, 2, 2 * P], F32, work + 88064)
        wf = sb("wf", [P, 2, P], F32, work + 90112)
        k2 = sb("k2", [P, 2, 2, TOK], F32R, work + 12288)
        q2 = sb("q2", [P, 2, 3, TOK], F32R, work + 24576)
        prob = sb("prob", [P, P_RING, TOK], F32, work + 43008)
        diag = sb("diag", [P, 2, 3, P], F32, work + 52224)
        pth = sb("pth", [P, 2, 6, 3 * P], F32R, work + 55296)
        ptl = sb("ptl", [P, 2, 6, 3 * P], F32R, work + 73728)
        corr = acc[:].rearrange("p (s n) -> p s n", s=2)
        osum = rstd[:].rearrange("p (s n) -> p s n", s=2)

        scratch = nc.dram_tensor("qk_parts", [8, 2, P, TOK], F32).ap()

        ring = [ctx.enter_context(nc.psum_tensor(f"ring{i}", [P, 1024], F32)) for i in range(2)]
        side = ctx.enter_context(nc.psum_tensor("side", [P, 1024], F32))
        bank = [ctx.enter_context(nc.psum_tensor(f"bank{i}", [P, 512], F32)) for i in range(2)]

        const_loaded, more_loaded = sem("const_loaded"), sem("more_loaded")
        h_loaded = sem("h_loaded")
        w_loaded = [sem("w_loaded_even"), sem("w_loaded_odd")]
        whi_ready, wlo_ready, mm_done = sem("whi_ready"), sem("wlo_ready"), sem("mm_done")
        consts_ready = sem("consts_ready")
        cond_ready, sink_ready = sem("cond_ready"), sem("sink_ready")
        ada_first_loaded = [sem(f"ada_first_loaded{i}") for i in range(4)]
        ada_loaded = sem("ada_loaded")
        ada_lat_done, ada_prod_done, ada_ctx_done = sem("ada_lat_done"), sem("ada_prod_done"), sem("ada_ctx_done")
        ada_turned, ada_red_done = sem("ada_turned"), sem("ada_red_done")
        ada_row_mm, ada_row_read, first_turned = sem("ada_row_mm"), sem("ada_row_read"), sem("first_turned")
        gate_ready = sem("gate_ready")
        silu_done, prod_done, ahi_done, alo_done = sem("silu_done"), sem("prod_done"), sem("ahi_done"), sem("alo_done")
        resid_done, sq_done, acc_done, ssq_ready = sem("resid_done"), sem("sq_done"), sem("acc_done"), sem("ssq_ready")
        std_done, rstd_ready, vec_ready = sem("std_done"), sem("rstd_ready"), sem("vec_ready")
        t1_ready, mod_done, x_ready = sem("t1_ready"), sem("mod_done"), sem("x_ready")
        pos_loaded = sem("pos_loaded")
        tab_loaded, wf_zeroed, wf_loaded = sem("tab_loaded"), sem("wf_zeroed"), sem("wf_loaded")
        evac_done, four_mm, four_ready = sem("evac_done"), sem("four_mm"), sem("four_ready")
        v_turned, vhi_done, v_ready = sem("v_turned"), sem("vhi_done"), sem("v_ready")
        f1_done, v1_even, v1_odd = sem("f1_done"), sem("v1_even"), sem("v1_odd")
        f2_done = sem("f2_done")
        bn_done, bstd_done, brstd_done, unorm_done = sem("bn_done"), sem("bstd_done"), sem("brstd_done"), sem("unorm_done")
        sqh_done, rot_done, rope_done, qhi_done, qlo_done = sem("sqh_done"), sem("rot_done"), sem("rope_done"), sem("qhi_done"), sem("qlo_done")
        stored = [sem("stored_even"), sem("stored_odd")]
        stack_loaded = [sem("stack_loaded_even"), sem("stack_loaded_odd")]
        sc_done, max_done, nm_ready, exp_done = sem("sc_done"), sem("max_done"), sem("nm_ready"), sem("exp_done")
        tot_done, inv_ready, diag_done = sem("tot_done"), sem("inv_ready"), sem("diag_done")
        sink_exp_done = sem("sink_exp_done")
        p_turned, pth_done, pt_ready, pv_done = sem("p_turned"), sem("pth_done"), sem("pt_ready"), sem("pv_done")
        oadd_done = sem("oadd_done")
        corr_done, osum_done, ohi_done, mix_ready = sem("corr_done"), sem("osum_done"), sem("ohi_done"), sem("mix_ready")
        fhi_done = sem("fhi_done")
        out_ready, out_stored = sem("out_ready"), sem("out_stored")

        CONSTS = 11

        def slot_free(eng, r, i=None, first=0):
            if r < 2:
                return
            name, value = plan.release[r - 2]
            if i is None:
                eng.wait_ge(sem_of[name], value)
            else:
                step = plan.release[r][1] - value
                assert plan.release[r][0] == name
                eng.wait_ge(sem_of[name], (i - first) * step + value)

        def tile_sizes(s):
            return ([KD] * (W_IN_TILES + W_OUT_TILES) if s["kind"] == "mix"
                    else ([KD] * 2 * GF + [GF] * KD) * GROUPS)

        NK = [nk for s in stages for nk in tile_sizes(s)]
        N_TILES = len(NK)

        def mix_counts(layer):
            before = sum(2 + len(score_tiles(l)) // 3 for l in range(layer))
            per = len(score_tiles(layer)) // 6
            return before + 2, before + 2 + per, before + 2 + 2 * per

        block = ctx.enter_context(nc.Block())

        @block.sync
        def _(sp):
            sp.dma_start(cond[:], c_cols).then_inc(const_loaded, 16)
            sp.dma_start(bias_ada[:], b_ada).then_inc(const_loaded, 16)
            for u in range(FIRST_UNITS):
                if u >= 4:
                    sp.wait_ge(ada_row_mm, u - 3)
                sp.dma_start(ada_first[u % 4][:], w_ada[u]).then_inc(ada_first_loaded[u % 4], 16)
                if u == 0:
                    sp.dma_start(h[:, :, 0:SEQ], x_t).then_inc(h_loaded, 16)
                    sp.dma_start(h[:, :, SEQ:TOK], ctx_t).then_inc(h_loaded, 16)
                    for dst, src in ((gain, gains), (gain_final, g_final), (qkg, qk_gain), (sinks, sink),
                                     (chan, dft_chan)):
                        sp.dma_start(dst[:], src).then_inc(more_loaded, 16)

            def load_w(t, slot, src, nk):
                if not isinstance(t, int) or t >= 2:
                    sp.wait_ge(wlo_ready, t - 1)
                sp.dma_start(raw[:, slot, 0:nk * P], src).then_inc(w_loaded[slot], 16)

            def load_ada(u):
                if not isinstance(u, int) or u > 0:
                    sp.wait_ge(ada_lat_done, u * KD)
                    sp.wait_ge(ada_prod_done, u * KD)
                sp.dma_start(ada_buf[:], w_ada[u + FIRST_UNITS]).then_inc(ada_loaded, 16)

            for s in stages:
                layer, n = s["layer"], s["n"]
                if s["kind"] == "mix":
                    load_w(s["t"], 0, w_in[layer, 0], KD)
                    load_w(s["t"] + 1, 1, w_in[layer, 1], KD)
                    load_w(s["t"] + 2, 0, w_in[layer, 2], KD)
                    load_w(s["t"] + 3, 1, w_in[layer, 3], KD)
                    sp.wait_ge(x_ready, KD * (n + 1))
                    sp.dma_start(rope_tab[:], rope).then_inc(tab_loaded, 16)
                    sp.wait_ge(wf_zeroed, layer + 1)
                    for g in range(4):
                        a = HD * (g % 2)
                        sp.dma_start(wf[a:a + HD, g // 2, a:a + HD], w_four[layer, g]).then_inc(wf_loaded, 16)

                    def store(q):
                        width = w_in_width(layer, q)
                        sp.wait_ge(qlo_done, 8 * layer + q + 1)
                        sp.dma_start(scratch[q, 0, :, 0:width], qkh[:, q % 2, 0:width].bitcast(F32)).then_inc(stored[q % 2], 16)
                        sp.dma_start(scratch[q, 1, :, 0:width], qkl[:, q % 2, 0:width].bitcast(F32)).then_inc(stored[q % 2], 16)

                    def load_stack(z):
                        branch, kv, slot = z // 2, z % 2, z % 2
                        first = (QA if branch == 0 else QB)[0]
                        chunks = slice(first, first + 3)
                        width = w_in_width(layer, QA[0])
                        sp.wait_ge(stored[0], 32 * 4 * (layer + 1))
                        sp.wait_ge(stored[1], 32 * 4 * (layer + 1))
                        if z >= 2:
                            sp.wait_ge(sc_done, s["scores"] + len(s["tiles"]) // 4 * (z - 1))
                        rows = slice(kv * HD, kv * HD + HD)
                        for half in range(2):
                            part = slice(half * HD, half * HD + HD)
                            sp.dma_start(k2[part, slot, :, :].bitcast(F32),
                                         scratch[KA if branch == 0 else KB, :, rows, :].rearrange("x p c -> p x c")).then_inc(stack_loaded[slot], 16)
                            sp.dma_start(q2[part, slot, :, 0:width].bitcast(F32),
                                         scratch[chunks, half, rows, 0:width].rearrange("g p c -> p g c")).then_inc(stack_loaded[slot], 16)

                    for j in range(4, W_IN_TILES):
                        load_w(s["t"] + j, j % 2, w_in[layer, j], KD)
                        if j == 6:
                            sp.dma_start(pos_lat[:], dft_lat).then_inc(pos_loaded, 16)
                            sp.dma_start(pos_ctx[:], dft_ctx).then_inc(pos_loaded, 16)
                        if 5 <= j:
                            store(j - 5)
                    load_w(s["t"] + 12, 0, w_out[layer, 0], KD)
                    store(7)
                    load_stack(0)
                    load_stack(1)
                    load_w(s["t"] + 13, 1, w_out[layer, 1], KD)
                    load_stack(2)
                    load_stack(3)
                    for d in range(2, W_OUT_TILES):
                        load_w(s["t"] + 12 + d, d % 2, w_out[layer, d], KD)
                    continue
                j = 2 * layer + (s["kind"] == "ffn2")
                for g in range(GROUPS):
                    t = s["t"] + g * (2 * GF + KD)
                    u0, nu = plan.ada.get((n, g), (0, 0))
                    for u in range(2):
                        load_w(t + u, u, w_gu[j, g * GF, u], KD)
                    if nu:
                        a = 1
                        if u0 == 0:
                            for u in range(2):
                                load_w(t + u + 2, u, w_gu[j, 1, u], KD)
                            load_ada(0)
                            a = 2
                        with sp.Fori(a, 1 + nu) as i:
                            for u in range(2):
                                load_w(t + u + 2 * i, u, w_gu[j, g * GF + i, u], KD)
                            load_ada(i + (u0 - 1))
                    with sp.Fori(1 + nu, GF) as i:
                        for u in range(2):
                            load_w(t + u + 2 * i, u, w_gu[j, g * GF + i, u], KD)
                    t += 2 * GF
                    with sp.Fori(0, KD // 2) as i:
                        for u in range(2):
                            load_w(t + u + 2 * i, u, w_down[j, g, 2 * i + u], GF)
            sp.wait_ge(stored[0], 32 * 4 * DEPTH)
            sp.wait_ge(stored[1], 32 * 4 * DEPTH)
            for d in range(KD):
                sp.wait_ge(out_ready, d + 1)
                sp.dma_start(out[:, d, :], h[:, d, 0:SEQ]).then_inc(out_stored, 16)
            sp.wait_ge(out_stored, 16 * KD)

        @block.gpsimd
        def _(pool):
            pool.memset(ones[:], 1.0).then_inc(consts_ready, 1)
            pool.memset(head_ones[:], 0.0).then_inc(consts_ready, 1)
            pool.memset(ident[:], 0.0).then_inc(consts_ready, 1)
            pool.memset(ident_b[:], 0.0).then_inc(consts_ready, 1)
            pool.memset(band_mask[:], 0.0).then_inc(consts_ready, 1)
            pool.memset(eps[:], NORM_EPS).then_inc(consts_ready, 1)
            pool.wait_ge(consts_ready, 6)
            pool.memset(head_ones[0:HD, 0:HD], 1.0).then_inc(consts_ready, 1)
            pool.wait_ge(consts_ready, 7)
            pool.memset(head_ones[HD:P, HD:P], 1.0).then_inc(consts_ready, 1)
            pool.wait_ge(consts_ready, 8)
            for m in (ident, ident_b):
                pool.affine_select(out=m[:], in_=m[:], compare_op=ALU.not_equal, fill=1.0, base=0,
                                   pattern=[[-1, P]], channel_multiplier=1).then_inc(consts_ready, 1)
            pool.affine_select(out=band_mask[:, 0], in_=band_mask[:, 0], compare_op=ALU.is_ge, fill=NEG_INF,
                               base=0, pattern=[[1, P]], channel_multiplier=-1)
            pool.affine_select(out=band_mask[:, 1], in_=band_mask[:, 1], compare_op=ALU.is_ge, fill=NEG_INF,
                               base=0, pattern=[[-1, P]], channel_multiplier=1).then_inc(consts_ready, 1)

            def ada_ctx(u):
                for k in range(1, KD):
                    pool.wait_ge(ada_prod_done, u * KD + k + 1)
                    if k == 1:
                        if not isinstance(u, int) or u > 0:
                            pool.wait_ge(ada_turned, u)
                        pool.tensor_tensor(ada_acc[:, 1], ada_tmp[:, 0], ada_tmp[:, 1], ALU.add).then_inc(ada_ctx_done, 2)
                    else:
                        pool.wait_ge(ada_ctx_done, u * KD + k)
                        pool.tensor_tensor(ada_acc[:, 1], ada_acc[:, 1], ada_tmp[:, k % 2], ALU.add).then_inc(ada_ctx_done, 1)

            def sum_squares(n, width):
                for d in range(KD - 1):
                    pool.wait_ge(sq_done, KD * n + d + 1)
                    if d == 0:
                        if n > 0:
                            pool.wait_ge(ssq_ready, n)
                        pool.tensor_copy(acc[:, 0:width], sq[:, 0, 0:width]).then_inc(acc_done, 1)
                    else:
                        pool.wait_ge(acc_done, (KD - 1) * n + d)
                        pool.tensor_tensor(acc[:, 0:width], acc[:, 0:width], sq[:, d % 2, 0:width], ALU.add).then_inc(acc_done, 1)

            sum_squares(0, TOK)
            for s in stages:
                layer, n, ow = s["layer"], s["n"], s["out_width"]
                if s["kind"] == "mix":
                    pool.wait_ge(x_ready, KD * (n + 1))
                    pool.memset(wf[:], 0.0).then_inc(wf_zeroed, 1)
                    pool.wait_ge(tab_loaded, 16 * (layer + 1))
                    for q in range(8):
                        g, sl, width = 8 * layer + q, q % 2, w_in_width(layer, q)
                        pool.wait_ge(rot_done, g + 1)
                        if q >= 2:
                            pool.wait_ge(qlo_done, g - 1)
                        if width == TOK:
                            pool.tensor_copy(roped[:, sl, SEQ:TOK], un[:, sl, SEQ:TOK])
                        pool.tensor_tensor(rot[:, sl], rot[:, sl], rope_tab[:, 1], ALU.mult).then_inc(rope_done, 1)
                        pool.wait_ge(rope_done, 2 * g + 1)
                        pool.tensor_tensor(roped[:, sl, 0:SEQ], rot[:, sl], ucos[:, sl], ALU.add).then_inc(rope_done, 1)
                    for i, (b, kv, q, g) in enumerate(s["tiles"]):
                        si = s["scores"] + i
                        if i == 0:
                            pool.wait_ge(f1_done, 6 * (layer + 1))
                        if g == 0 and i >= 6:
                            pool.wait_ge(pv_done, si // 3 - 1)
                        pool.wait_ge(inv_ready, si + 1)
                        pool.tensor_scalar(diag[:, i // 3 % 2, g], ident[:], row_inv[:, i % 8:i % 8 + 1], None,
                                           ALU.mult).then_inc(diag_done, 1)
                    sum_squares(n + 1, ow)
                    continue
                for g in range(GROUPS):
                    u0, nu = plan.ada.get((n, g), (0, 0))
                    if nu:
                        if u0 == 0:
                            ada_ctx(0)
                        with pool.Fori(max(u0, 1), u0 + nu) as i:
                            ada_ctx(i)
                sum_squares(n + 1, ow)

        def act_w_in(act, s, split_hi):
            layer, t = s["layer"], s["t"]
            e0, q0 = W_IN_TILES * layer, 8 * layer
            act.preload_act_table(ACT.Sqrt)

            def round_qk(q):
                width = w_in_width(layer, q)
                act.wait_ge(rope_done, 2 * (q0 + q) + 2)
                if q0 + q >= 2:
                    act.wait_ge(stored[q % 2], 32 * ((q0 + q) // 2))
                act.activation(qkh[:, q % 2, 0:width], roped[:, q % 2, 0:width], ACT.Copy).then_inc(qhi_done, 1)

            def head_std(j):
                width = w_in_width(layer, j)
                act.wait_ge(bn_done, 4 * layer + j - KB + 1)
                if 4 * layer + j - KB >= 1:
                    act.wait_ge(unorm_done, 4 * layer + j - KB)
                act.activation(rstd[:, 0:width], side[:, 0:width], ACT.Sqrt, bias=eps[:], scale=1.0 / HD).then_inc(bstd_done, 1)

            def round_values(b):
                for half, (a, n_) in enumerate(((0, 4), (4, 2))):
                    act.wait_ge(v_turned, 4 * layer + 2 * b + half + 1)
                    for kv, col in ((0, 0), (1, 3 * HD)):
                        last = act.activation(v2[:, b, a:a + n_, col:col + HD],
                                              bank[half][:, 0:n_ * P].rearrange("p (n f) -> p n f", f=P)[:, :, kv * HD:kv * HD + HD], ACT.Copy)
                    last.then_inc(vhi_done, 1)

            for j in range(W_IN_TILES):
                tt = t + j
                width = w_in_width(layer, j)
                if j > 0:
                    split_hi(tt + 1, (tt + 1) % 2, NK[tt + 1])
                if j == 2:
                    act.wait_ge(four_mm, layer + 1)
                    act.activation(four[:].rearrange("p c n -> p (c n)"), bank[0][:, 0:4 * P], ACT.Copy).then_inc(four_ready, 1)
                if j == UF[1]:
                    round_values(0)
                act.wait_ge(mm_done, tt + 1)
                if j in UF:
                    act.activation(uf[:, j % 2, 0:width], ring[j % 2][:, 0:width], ACT.Copy).then_inc(evac_done, 1)
                else:
                    if j >= 2:
                        act.wait_ge(rope_done, 2 * (q0 + j - 2) + 2)
                    last = act.activation(un[:, j % 2, 0:width], ring[j % 2][:, 0:width], ACT.Copy)
                    if j not in (KB,) + QB:
                        last.then_inc(evac_done, 1)
                    else:
                        if j > KB:
                            head_std(j - 1)
                        act.activation(acc[:, 0:width], ring[j % 2][:, 0:width], ACT.Square).then_inc(evac_done, 1)
                    if j == QB[2] + 1:
                        head_std(QB[2])
                        act.preload_act_table(ACT.Exp)
                if 0 <= j - 2 < ROPED:
                    round_qk(j - 2)
            round_values(1)

        def act_fourier(act, layer):
            for blk in (0, 2, 4):
                act.wait_ge(f1_done, 6 * layer + blk + 1)
                act.activation(v1[:, blk].rearrange("p c n -> p (c n)"), bank[0][:, 0:4 * P], ACT.Copy).then_inc(v1_even, 1)
            for c in range(2):
                wd = w_in_width(layer, UF[0])
                act.wait_ge(f2_done, 2 * layer + c + 1)
                act.activation(xh[:, 6 + c, 0:wd], side[:, 0:wd], ACT.Copy).then_inc(fhi_done, 1)

        @block.scalar
        def _(act):
            def split_hi(t, slot, nk):
                if isinstance(t, int):
                    act.wait_ge(w_loaded[slot], 16 * (t // 2 + 1))
                else:
                    act.wait_ge(w_loaded[slot], (t + (2 - slot)) * 8)
                if not isinstance(t, int) or t >= 2:
                    act.wait_ge(mm_done, t - 1)
                act.activation(whi[:, slot, 0:nk * P], raw[:, slot, 0:nk * P], ACT.Copy).then_inc(whi_ready, 1)

            def ada_products(u, ks):
                if ks[0] == 0:
                    act.wait_ge(ada_loaded, (u + 1) * 16)
                for k in ks:
                    if not isinstance(u, int) or u * KD + k >= 2:
                        act.wait_ge(ada_ctx_done, u * KD + (k - 1))
                    act.activation(ada_tmp[:, k % 2], ada_buf[:, k], ACT.Copy, scale=scond[:, 1, k:k + 1]).then_inc(ada_prod_done, 1)

            def square(n, d, width):
                if d >= 2:
                    act.wait_ge(acc_done, (KD - 1) * n + d - 1)
                act.activation(sq[:, d % 2, 0:width], h[:, d, 0:width], ACT.Square).then_inc(sq_done, 1)

            def norm(n, width, layer, stage):
                if layer is not None:
                    split_hi(stages[n]["t"] + 1, 1, KD)
                act.wait_ge(ssq_ready, n + 1)
                act.activation(rstd[:, 0:width], side[:, 0:width], ACT.Sqrt, bias=eps[:], scale=1.0 / D_MODEL).then_inc(std_done, 1)
                if layer is None:
                    return
                if stage != 1:
                    act.preload_act_table(ACT.Silu)
                act.wait_ge(vec_ready, 2 * (n + 1))
                for d in range(KD):
                    act.wait_ge(t1_ready, KD * n + d + 1)
                    for c, (a, b) in enumerate(spans(width)):
                        col = MODC * layer + 3 * KD * stage + d
                        last = act.activation(xh[:, d, a:b], t1[:, d % 4, a:b], ACT.Identity, bias=modv[:, c, col:col + 1])
                    last.then_inc(mod_done, 1)

            act.preload_act_table(ACT.Silu)
            act.wait_ge(const_loaded, 16 * 2)
            act.activation(scond[:], cond[:], ACT.Silu).then_inc(cond_ready, 1)
            act.preload_act_table(ACT.Sqrt)
            for u in range(FIRST_UNITS):
                act.wait_ge(ada_row_mm, u + 1)
                if u >= 2:
                    act.wait_ge(first_turned, u - 1)
                act.activation(ada_rows[:, u % 2], bank[u % 2][0:2, 0:ADA_COLS], ACT.Copy).then_inc(ada_row_read, 1)
            act.wait_ge(consts_ready, CONSTS)
            act.wait_ge(more_loaded, 16 * 5)
            act.activation(sinks8[:], sinks[:], ACT.Copy, scale=1.0 / SCALE).then_inc(sink_ready, 1)
            split_hi(0, 0, NK[0])
            act.wait_ge(h_loaded, 32)
            for d in range(KD):
                square(0, d, TOK)
            norm(0, TOK, 0, 0)

            for s in stages:
                layer, n, width, ow = s["layer"], s["n"], s["width"], s["out_width"]
                t = s["t"]
                if s["kind"] == "mix":
                    act_w_in(act, s, split_hi)
                    tiles = s["tiles"]
                    for i in range(len(tiles) + LAG + 6):
                        if i == 2:
                            act_fourier(act, layer)
                        j = i - LAG
                        if 0 <= j < len(tiles):
                            b, kv, q, g = tiles[j]
                            sj, tr = s["scores"] + j, (s["scores"] + j) // 3
                            nb = len(key_blocks(b, q)) + 2
                            act.wait_ge(p_turned, sj + 1)
                            if g == 0 and j // 3 >= 2:
                                act.wait_ge(pv_done, tr - 1)
                            act.activation(pth[:, j // 3 % 2, 0:nb, g * P:(g + 1) * P],
                                           side[:, 0:nb * P].rearrange("p (n q) -> p n q", q=P), ACT.Copy).then_inc(pth_done, 1)
                        k = i - LAG - 5
                        if k >= 0 and k % 3 == 0 and k // 3 < len(tiles) // 3:
                            b, kv, q, g = tiles[k]
                            tr = s["scores"] // 3 + k // 3
                            here, there = slice(kv * HD, kv * HD + HD), slice((1 - kv) * HD, (1 - kv) * HD + HD)
                            act.wait_ge(pv_done, tr + 1)
                            act.activation(corr[here, k // 3 % 2], bank[0][there, 0:3 * P], ACT.Copy).then_inc(corr_done, 1)
                        if i < len(tiles):
                            b, kv, q, g = tiles[i]
                            si = s["scores"] + i
                            lo = SEQ - P * len(key_blocks(b, q))
                            act.wait_ge(nm_ready, si + 1)
                            if i == 2:
                                act.wait_ge(f1_done, 6 * (layer + 1))
                            if i >= P_RING:
                                act.wait_ge(p_turned, si - P_RING + 1)
                            act.activation(prob[:, i % P_RING, lo:TOK], ring[(s["r"] + W_IN_TILES + i) % 2][:, lo:TOK], ACT.Exp,
                                           bias=neg_max[:, i % 4:i % 4 + 1], scale=SCALE,
                                           accum_out=row_sum[:, i % 4:i % 4 + 1]).then_inc(exp_done, 1)
                            if b == 0:
                                sc = 6 * layer + 3 * kv + g
                                act.activation(sink_exp[:, i % 4:i % 4 + 1], sinks[:, sc:sc + 1], ACT.Exp,
                                               bias=neg_max[:, i % 4:i % 4 + 1], scale=1.0).then_inc(sink_exp_done, 1)
                        k = i - LAG - 6
                        if k >= 0 and k % 3 == 0 and k // 3 < len(tiles) // 3:
                            b, kv, q, g = tiles[k]
                            tr = s["scores"] // 3 + k // 3
                            here = slice(kv * HD, kv * HD + HD)
                            act.wait_ge(osum_done, tr + 1)
                            act.activation(xh[here, 3 * b:3 * b + 3, q * P:(q + 1) * P],
                                           osum[here, k // 3 % 2].rearrange("p (g q) -> p g q", q=P), ACT.Copy).then_inc(ohi_done, 1)
                    act.preload_act_table(ACT.Sqrt)
                    for d in range(W_OUT_TILES):
                        tt = t + W_IN_TILES + d + 1
                        split_hi(tt, tt % 2, NK[tt])
                        act.wait_ge(resid_done, s["resid"] + d + 1)
                        square(n + 1, d, ow)
                    norm(n + 1, stages[n + 1]["width"], layer, 2)
                    continue
                for g in range(GROUPS):
                    p0 = s["pairs"] + g * GF

                    def pair(tt, f, pi, nk_next, split=True, u=None):
                        if split:
                            split_hi(tt + 1, 1, KD)
                        if u is not None:
                            ada_products(u, range(0, KD // 2))
                        act.wait_ge(mm_done, tt + 1)
                        if not isinstance(pi, int) or pi > 0:
                            act.wait_ge(prod_done, pi)
                        act.activation(sil[:, 0:width], ring[0][:, 0:width], ACT.Silu).then_inc(silu_done, 1)
                        split_hi(tt + 2, 0, nk_next)
                        if u is not None:
                            ada_products(u, range(KD // 2, KD))
                        act.wait_ge(prod_done, pi + 1)
                        act.activation(ah[:, f, 0:width], atmp[:, 0:width], ACT.Copy).then_inc(ahi_done, 1)

                    u0, nu = plan.ada.get((n, g), (0, 0))
                    act.preload_act_table(ACT.Silu)
                    pair(t, 0, p0, KD, split=g > 0)
                    if nu:
                        if u0 == 0:
                            pair(t + 2, 1, p0 + 1, KD, u=0)
                        with act.Fori(2 if u0 == 0 else 1, 1 + nu) as i:
                            pair(t + 2 * i, i, p0 + i, KD, u=i + (u0 - 1))
                    if 1 + nu < GF - 1:
                        with act.Fori(1 + nu, GF - 1) as i:
                            pair(t + 2 * i, i, p0 + i, KD)
                    pair(t + 2 * GF - 2, GF - 1, p0 + GF - 1, GF)
                    t += 2 * GF
                    if g == 0:
                        with act.Fori(0, KD // 2 - 1) as i:
                            for u in range(2):
                                split_hi(t + u + 2 * i + 1, 1 - u, GF)
                        split_hi(t + KD - 1, 1, GF)
                        split_hi(t + KD, 0, KD)
                    else:
                        act.preload_act_table(ACT.Sqrt)
                        for d in range(KD):
                            if t + d + 1 < N_TILES:
                                split_hi(t + d + 1, (d + 1) % 2, NK[t + d + 1])
                            act.wait_ge(resid_done, s["resid"] + KD + d + 1)
                            square(n + 1, d, ow)
                    t += KD
                if n + 1 < len(stages):
                    nx = stages[n + 1]
                    norm(n + 1, nx["width"], nx["layer"], 1 if nx["kind"] == "mix" else 0)
                else:
                    norm(n + 1, SEQ, None, None)

        def dve_w_in(dve, s, split_lo):
            layer, t = s["layer"], s["t"]
            e0, q0 = W_IN_TILES * layer, 8 * layer

            def head_norm_rope(j):
                sl, width = j % 2, w_in_width(layer, j)
                if j < KA:
                    b = 4 * layer + j - KB
                    dve.wait_ge(bstd_done, b + 1)
                    dve.reciprocal(rstd[:, 0:width], rstd[:, 0:width]).then_inc(brstd_done, 1)
                    dve.wait_ge(brstd_done, b + 1)
                    kq = 2 * layer + (1 if j == KB else 0)
                    dve.scalar_tensor_tensor(out=un[:, sl, 0:width], in0=un[:, sl, 0:width], scalar=qkg[:, kq:kq + 1],
                                             in1=rstd[:, 0:width], op0=ALU.mult, op1=ALU.mult).then_inc(unorm_done, 1)
                    dve.wait_ge(unorm_done, b + 1)
                dve.wait_ge(evac_done, e0 + j + 1)
                if j == 0:
                    dve.wait_ge(tab_loaded, 16 * (layer + 1))
                dve.stream_shuffle(rot[:, sl], un[:, sl, 0:SEQ], [i ^ 16 for i in range(32)])
                dve.tensor_tensor(ucos[:, sl], un[:, sl, 0:SEQ], rope_tab[:, 0], ALU.mult).then_inc(rot_done, 1)

            def rest_qk(q):
                width = w_in_width(layer, q)
                dve.wait_ge(qhi_done, q0 + q + 1)
                dve.tensor_tensor(qkl[:, q % 2, 0:width], roped[:, q % 2, 0:width], qkh[:, q % 2, 0:width].bitcast(F32),
                                  ALU.subtract).then_inc(qlo_done, 1)

            def rest_values(b):
                for half, (a, n_) in enumerate(((0, 4), (4, 2))):
                    dve.wait_ge(vhi_done, 4 * layer + 2 * b + half + 1)
                    for kv, hi, lo in ((0, 0, HD), (1, 3 * HD, 2 * HD)):
                        last = dve.tensor_tensor(
                            v2[:, b, a:a + n_, lo:lo + HD],
                            bank[half][:, 0:n_ * P].rearrange("p (n f) -> p n f", f=P)[:, :, kv * HD:kv * HD + HD],
                            v2[:, b, a:a + n_, hi:hi + HD].bitcast(F32), ALU.subtract)
                    last.then_inc(v_ready, 1)

            for j in range(W_IN_TILES):
                if j > 0:
                    split_lo(t + j + 1, (t + j + 1) % 2, NK[t + j + 1])
                if j == UF[1]:
                    rest_values(0)
                if 0 <= j - 1 < ROPED:
                    head_norm_rope(j - 1)
                if 0 <= j - 2 < ROPED:
                    rest_qk(j - 2)
            rest_values(1)

        def dve_fourier(dve, layer):
            for blk in (1, 3, 5):
                dve.wait_ge(f1_done, 6 * layer + blk + 1)
                dve.tensor_copy(v1[:, blk].rearrange("p c n -> p (c n)"), bank[1][:, 0:4 * P]).then_inc(v1_odd, 1)
            for c in range(2):
                wd = w_in_width(layer, UF[0])
                dve.wait_ge(fhi_done, 2 * layer + c + 1)
                dve.tensor_tensor(xl[:, 6 + c, 0:wd], side[:, 0:wd], xh[:, 6 + c, 0:wd].bitcast(F32), ALU.subtract).then_inc(mix_ready, 1)

        def dve_attention(dve, s):
            layer, tiles = s["layer"], s["tiles"]
            sinks_before = len(tiles) // 2 and sum(len(score_tiles(l)) // 2 for l in range(layer))
            for i in range(len(tiles) + LAG + 6):
                if i == 2:
                    dve_fourier(dve, layer)
                if i < len(tiles):
                    b, kv, q, g = tiles[i]
                    si = s["scores"] + i
                    lo = SEQ - P * len(key_blocks(b, q))
                    dve.wait_ge(sc_done, si + 1)
                    dve.reduce_max(row_max[:, i % 2:i % 2 + 1], ring[(s["r"] + W_IN_TILES + i) % 2][:, lo:TOK], AX.X).then_inc(max_done, 1)
                    dve.wait_ge(max_done, si + 1)
                    m, nm = row_max[:, i % 2:i % 2 + 1], neg_max[:, i % 4:i % 4 + 1]
                    if b == 0:
                        if i == 0:
                            dve.wait_ge(sink_ready, 1)
                        sc = 6 * layer + 3 * kv + g
                        dve.tensor_scalar(nm, m, sinks8[:, sc:sc + 1], -SCALE, ALU.max, ALU.mult).then_inc(nm_ready, 1)
                    else:
                        dve.tensor_scalar(nm, m, -SCALE, None, ALU.mult).then_inc(nm_ready, 1)
                j = i - 1
                if 0 <= j < len(tiles):
                    b, kv, q, g = tiles[j]
                    sj = s["scores"] + j
                    tot = row_sum[:, j % 4:j % 4 + 1]
                    dve.wait_ge(exp_done, sj + 1)
                    if b == 0:
                        dve.wait_ge(sink_exp_done, sinks_before + j + 1)
                        dve.tensor_tensor(row_tot[:, j % 2:j % 2 + 1], tot, sink_exp[:, j % 4:j % 4 + 1], ALU.add).then_inc(tot_done, 1)
                        dve.wait_ge(tot_done, sinks_before + j + 1)
                        tot = row_tot[:, j % 2:j % 2 + 1]
                    if j >= 8:
                        dve.wait_ge(diag_done, sj - 7)
                    dve.reciprocal(row_inv[:, j % 8:j % 8 + 1], tot).then_inc(inv_ready, 1)
                j = i - LAG
                if 0 <= j < len(tiles):
                    b, kv, q, g = tiles[j]
                    sj = s["scores"] + j
                    nb = len(key_blocks(b, q)) + 2
                    dve.wait_ge(pth_done, sj + 1)
                    part = slice(g * P, (g + 1) * P)
                    dve.tensor_tensor(ptl[:, j // 3 % 2, 0:nb, part], side[:, 0:nb * P].rearrange("p (n q) -> p n q", q=P),
                                      pth[:, j // 3 % 2, 0:nb, part].bitcast(F32), ALU.subtract).then_inc(pt_ready, 1)
                k = i - LAG - 5
                if k >= 0 and k % 3 == 0 and k // 3 < len(tiles) // 3:
                    b, kv, q, g = tiles[k]
                    tr = s["scores"] // 3 + k // 3
                    here = slice(kv * HD, kv * HD + HD)
                    dve.wait_ge(corr_done, tr + 1)
                    o = osum[here, k // 3 % 2]
                    dve.tensor_tensor(o, bank[0][here, 0:3 * P], corr[here, k // 3 % 2], ALU.add).then_inc(oadd_done, 1)
                    dve.wait_ge(oadd_done, tr + 1)
                    dve.tensor_tensor(o, o, bank[1][here, 0:3 * P], ALU.mult).then_inc(osum_done, 1)
                k = i - LAG - 6
                if k >= 0 and k % 3 == 0 and k // 3 < len(tiles) // 3:
                    b, kv, q, g = tiles[k]
                    tr = s["scores"] // 3 + k // 3
                    here, cols = slice(kv * HD, kv * HD + HD), slice(q * P, (q + 1) * P)
                    dve.wait_ge(ohi_done, tr + 1)
                    dve.tensor_tensor(xl[here, 3 * b:3 * b + 3, cols], osum[here, k // 3 % 2].rearrange("p (g q) -> p g q", q=P),
                                      xh[here, 3 * b:3 * b + 3, cols].bitcast(F32), ALU.subtract).then_inc(mix_ready, 1)

        @block.vector
        def _(dve):
            def split_lo(t, slot, nk):
                dve.wait_ge(whi_ready, t + 1)
                dve.tensor_tensor(wlo[:, slot, 0:nk * P], raw[:, slot, 0:nk * P], whi[:, slot, 0:nk * P].bitcast(F32),
                                  ALU.subtract).then_inc(wlo_ready, 1)

            def ada_lat(u, ks):
                for k in ks:
                    if k == 0:
                        dve.wait_ge(ada_loaded, (u + 1) * 16)
                        if not isinstance(u, int) or u > 0:
                            dve.wait_ge(ada_turned, u)
                        dve.tensor_scalar(ada_acc[:, 0], ada_buf[:, 0], scond[:, 0, 0:1], None, ALU.mult).then_inc(ada_lat_done, 1)
                    else:
                        dve.wait_ge(ada_lat_done, u * KD + k)
                        dve.scalar_tensor_tensor(out=ada_acc[:, 0], in0=ada_buf[:, k], scalar=scond[:, 0, k:k + 1],
                                                 in1=ada_acc[:, 0], op0=ALU.mult, op1=ALU.add).then_inc(ada_lat_done, 1)

            def ada_reduce(u):
                dve.wait_ge(ada_turned, u + 1)
                for c in range(2):
                    dve.tensor_reduce(ada_sum[:, c], bank[c][:, 0:ADA_COLS].rearrange("p (n k) -> p n k", k=P), AX.X,
                                      ALU.add).then_inc(ada_red_done, 1)
                dve.wait_ge(ada_red_done, u * 4 + 4)
                for c in range(2):
                    cols = bass.ds((u + FIRST_UNITS) * UC, UC)
                    dve.tensor_tensor(modv[:, c, cols], ada_sum[:, c], bias_ada[:, cols], ALU.add).then_inc(ada_red_done, 1)

            def gates(n, layer, stage, units, gate_scale):
                dve.wait_ge(ada_red_done, 2 + 4 * (units - FIRST_UNITS))
                if n > 0:
                    dve.wait_ge(resid_done, stages[n]["resid"])
                col = MODC * layer + 3 * KD * stage
                for c in range(2):
                    dve.tensor_scalar(vec_gate[:, c], modv[:, c, col + 2 * KD:col + 3 * KD], gate_scale, None,
                                      ALU.mult).then_inc(gate_ready, 1)
                dve.wait_ge(gate_ready, 2 * (n + 1))

            def norm(n, width, layer, stage, units):
                if layer is not None:
                    dve.wait_ge(ada_red_done, 2 + 4 * (units - FIRST_UNITS if n > 0 else 0))
                    col = MODC * layer + 3 * KD * stage
                    for c in range(2):
                        dve.scalar_tensor_tensor(out=vec_scale[:, c], in0=modv[:, c, col + KD:col + 2 * KD], scalar=1.0,
                                                 in1=gain[:, 3 * layer + stage], op0=ALU.add, op1=ALU.mult).then_inc(vec_ready, 1)
                    if n > 0:
                        gates(n, layer, stage, units, 1.0 if stage == 1 else 0.5)
                    split_lo(stages[n]["t"] + 1, 1, KD)
                    dve.wait_ge(vec_ready, 2 * (n + 1))
                dve.wait_ge(std_done, n + 1)
                dve.reciprocal(rstd[:, 0:width], rstd[:, 0:width]).then_inc(rstd_ready, 1)
                dve.wait_ge(rstd_ready, n + 1)
                if layer is None:
                    for d in range(KD):
                        dve.scalar_tensor_tensor(out=h[:, d, 0:SEQ], in0=h[:, d, 0:SEQ], scalar=gain_final[:, d:d + 1],
                                                 in1=rstd[:, 0:SEQ], op0=ALU.mult, op1=ALU.mult).then_inc(out_ready, 1)
                    return
                for d in range(KD + 1):
                    if d < KD:
                        if d >= 4:
                            dve.wait_ge(x_ready, KD * n + d - 3)
                        for c, (a, b) in enumerate(spans(width)):
                            last = dve.scalar_tensor_tensor(out=t1[:, d % 4, a:b], in0=h[:, d, a:b], scalar=vec_scale[:, c, d:d + 1],
                                                            in1=rstd[:, a:b], op0=ALU.mult, op1=ALU.mult)
                        last.then_inc(t1_ready, 1)
                    if d >= 1:
                        e = d - 1
                        dve.wait_ge(mod_done, KD * n + d)
                        for c, (a, b) in enumerate(spans(width)):
                            shift = MODC * layer + 3 * KD * stage + e
                            last = dve.scalar_tensor_tensor(out=xl[:, e, a:b], in0=t1[:, e % 4, a:b], scalar=modv[:, c, shift:shift + 1],
                                                            in1=xh[:, e, a:b].bitcast(F32), op0=ALU.add, op1=ALU.subtract)
                        last.then_inc(x_ready, 1)

            def residual(t_done, d, slot, width):
                dve.wait_ge(mm_done, t_done)
                for c, (a, b) in enumerate(spans(width)):
                    last = dve.scalar_tensor_tensor(out=h[:, d, a:b], in0=ring[slot][:, a:b], scalar=vec_gate[:, c, d:d + 1],
                                                    in1=h[:, d, a:b], op0=ALU.mult, op1=ALU.add)
                last.then_inc(resid_done, 1)

            dve.wait_ge(const_loaded, 16 * 2)
            dve.wait_ge(more_loaded, 16 * 5)
            split_lo(0, 0, NK[0])
            dve.wait_ge(first_turned, FIRST_UNITS)
            for c in range(2):
                dve.tensor_tensor(modv[:, c, 0:FIRST_UNITS * UC], ring[1][:, 0:2 * FIRST_UNITS * UC].rearrange("p (m c) -> p c m", c=2)[:, c],
                                  bias_ada[:, 0:FIRST_UNITS * UC], ALU.add).then_inc(ada_red_done, 1)
            norm(0, TOK, 0, 0, None)

            for s in stages:
                layer, n, width, ow = s["layer"], s["n"], s["width"], s["out_width"]
                t = s["t"]
                if s["kind"] == "mix":
                    dve_w_in(dve, s, split_lo)
                    dve_attention(dve, s)
                    for d in range(W_OUT_TILES):
                        tt = t + W_IN_TILES + d
                        split_lo(tt + 1, (tt + 1) % 2, NK[tt + 1])
                        residual(tt + 1, d, (s["r"] + W_IN_TILES + len(s["tiles"]) + d) % 2, ow)
                    norm(n + 1, stages[n + 1]["width"], layer, 2, ADA_UNITS * (layer + 1))
                    continue
                for g in range(GROUPS):
                    p0 = s["pairs"] + g * GF

                    def pair(tt, f, pi, nk_next, split=True, u=None):
                        if split:
                            split_lo(tt + 1, 1, KD)
                        if u is not None:
                            ada_lat(u, range(0, KD // 2))
                        split_lo(tt + 2, 0, nk_next)
                        if u is not None:
                            ada_lat(u, range(KD // 2, KD))
                        dve.wait_ge(silu_done, pi + 1)
                        dve.wait_ge(mm_done, tt + 2)
                        dve.tensor_tensor(atmp[:, 0:width], sil[:, 0:width], ring[1][:, 0:width], ALU.mult).then_inc(prod_done, 1)
                        dve.wait_ge(ahi_done, pi + 1)
                        dve.tensor_tensor(al[:, f, 0:width], atmp[:, 0:width], ah[:, f, 0:width].bitcast(F32),
                                          ALU.subtract).then_inc(alo_done, 1)
                        if u is not None:
                            ada_reduce(u)

                    u0, nu = plan.ada.get((n, g), (0, 0))
                    pair(t, 0, p0, KD, split=g > 0)
                    if nu:
                        if u0 == 0:
                            pair(t + 2, 1, p0 + 1, KD, u=0)
                        with dve.Fori(2 if u0 == 0 else 1, 1 + nu) as i:
                            pair(t + 2 * i, i, p0 + i, KD, u=i + (u0 - 1))
                    if 1 + nu < GF - 1:
                        with dve.Fori(1 + nu, GF - 1) as i:
                            pair(t + 2 * i, i, p0 + i, KD)
                    pair(t + 2 * GF - 2, GF - 1, p0 + GF - 1, GF)
                    t += 2 * GF
                    if n == 0 and g == 0:
                        gates(0, 0, 0, UNITS_PER_STAGE, 0.5)
                    for d in range(KD):
                        if t + d + 1 < N_TILES:
                            split_lo(t + d + 1, (d + 1) % 2, NK[t + d + 1])
                        residual(t + d + 1, d, d % 2, width)
                    t += KD
                if n + 1 < len(stages):
                    nx = stages[n + 1]
                    stage = 1 if nx["kind"] == "mix" else 0
                    norm(n + 1, nx["width"], nx["layer"], stage, ADA_UNITS * nx["layer"] + UNITS_PER_STAGE * (stage + 1))
                else:
                    norm(n + 1, SEQ, None, None, None)

        def pe_mixer(pe, s, product, product_pair):
            layer, n, t, r, tiles = s["layer"], s["n"], s["t"], s["r"], s["tiles"]
            x_w = w_in_width(layer, UF[0])
            blocks = 6 if x_w == TOK else 4
            e0 = W_IN_TILES * layer

            def head_squares(j):
                b, width = 4 * layer + j - KB, w_in_width(layer, j)
                pe.wait_ge(evac_done, e0 + j + 1)
                if j > KB:
                    pe.wait_ge(bstd_done, b)
                for a, c in spans(width):
                    last = pe.matmul(side[:, a:c], head_ones[:], acc[:, a:c], start=True, stop=True)
                last.then_inc(bn_done, 1)

            def turn_values(b):
                pe.wait_ge(evac_done, e0 + VA + b + 1)
                for half, (a, n_) in enumerate(((0, 4), (4, 2))):
                    if b == 1:
                        pe.wait_ge(v_ready, 4 * layer + half + 1)
                    elif half == 0:
                        pe.wait_ge(four_ready, layer + 1)
                    for m in range(n_):
                        last = pe.transpose(bank[half][:, m * P:(m + 1) * P], un[:, b, (a + m) * P:(a + m + 1) * P], ident[:])
                    last.then_inc(v_turned, 1)

            def fourier():
                for blk in range(6):
                    if blk < 2:
                        pe.wait_ge(v_ready, 4 * layer + 3 + blk)
                    elif blk % 2 == 0:
                        pe.wait_ge(v1_even, 3 * layer + blk // 2)
                    else:
                        pe.wait_ge(v1_odd, 3 * layer + blk // 2)
                    src = blk if blk < blocks else 0
                    for c in range(2):
                        last = pe.matmul(bank[blk % 2][:, c * 2 * P:(c + 1) * 2 * P], uf[:, c, src * P:(src + 1) * P], four[:, c],
                                         start=True, stop=True)
                    last.then_inc(f1_done, 1)
                pe.wait_ge(v1_even, 3 * layer + 3)
                pe.wait_ge(v1_odd, 3 * layer + 3)
                pe.wait_ge(pos_loaded, 32 * (layer + 1))
                for c in range(2):
                    if c == 1:
                        pe.wait_ge(mix_ready, mix_counts(layer)[0] - 1)
                    for tab, b0, nb, (lo, hi) in ((pos_lat, 0, 4, (0, SEQ)), (pos_ctx, 4, 2, (SEQ, TOK)))[:2 if blocks == 6 else 1]:
                        for m in range(nb):
                            for part in range(2):
                                last = pe.matmul(side[:, lo:hi], v1[:, b0 + m, c, part * P:(part + 1) * P], tab[:, part, m],
                                                 start=(m == 0 and part == 0), stop=(m == nb - 1 and part == 1))
                    last.then_inc(f2_done, 1)

            for j in range(W_IN_TILES):
                slot_free(pe, r + j)
                if j == 0:
                    slot_free(pe, r + 1)
                    product_pair(n, t, TOK)
                elif j > 1:
                    pe.wait_ge(wlo_ready, t + j + 1)
                    product(ring[j % 2], j % 2, KD, xh, xl, w_in_width(layer, j))
                if j == 1:
                    pe.wait_ge(wf_loaded, 64 * (layer + 1))
                    pe.wait_ge(more_loaded, 16 * 5)
                    for c in range(2):
                        for part in range(2):
                            o = (2 * c + part) * P
                            last = pe.matmul(bank[0][:, o:o + P], chan[:, part], wf[:, c], start=True, stop=True)
                    last.then_inc(four_mm, 1)
                if 0 <= j - 1 <= QB[2]:
                    head_squares(j - 1)
                if j == UF[0]:
                    turn_values(0)
            turn_values(1)
            t += W_IN_TILES
            r += W_IN_TILES

            def scores(i):
                b, kv, q, g = tiles[i]
                keys = key_blocks(b, q)
                lo = SEQ - P * len(keys)
                z = i // (len(tiles) // 4)
                out = ring[(r + i) % 2]
                slot_free(pe, r + i)
                if i % (len(tiles) // 4) == 0:
                    pe.wait_ge(stack_loaded[z % 2], 64 * (2 * layer + z // 2 + 1))
                query = q2[:, z % 2, g, q * P:(q + 1) * P]
                if keys:
                    k0 = keys[0] * P
                    edges = []
                    if b == 0:
                        if keys[0] == q - 1:
                            edges.append((0, lo))
                        if keys[-1] == q + 1:
                            edges.append((1, SEQ - P))
                    for part in range(2):
                        pe.matmul(out[:, lo:SEQ], query, k2[:, z % 2, part, k0:k0 + SEQ - lo], start=(part == 0),
                                  stop=(part == 1 and not edges))
                    for m, (e, col) in enumerate(edges):
                        pe.matmul(out[:, col:col + P], ident_b[:], band_mask[:, e], start=False, stop=(m == len(edges) - 1))
                for part in range(2):
                    last = pe.matmul(out[:, SEQ:TOK], query, k2[:, z % 2, part, SEQ:TOK], start=(part == 0), stop=(part == 1))
                last.then_inc(sc_done, 1)

            def turn_probs(i):
                b, kv, q, g = tiles[i]
                si = s["scores"] + i
                nb = len(key_blocks(b, q)) + 2
                lo = TOK - nb * P
                pe.wait_ge(exp_done, si + 1)
                if i >= 1:
                    pe.wait_ge(pt_ready, si)
                else:
                    pe.wait_ge(mix_ready, mix_counts(layer)[0])
                for m in range(nb):
                    last = pe.transpose(side[:, m * P:(m + 1) * P], prob[:, i % P_RING, lo + m * P:lo + (m + 1) * P], ident[:])
                last.then_inc(p_turned, 1)

            def weigh_values(k, half):
                b, kv, q, g = tiles[3 * k]
                tr = s["scores"] // 3 + k
                keys = key_blocks(b, q) + [4, 5]
                if half == 0:
                    pe.wait_ge(pt_ready, s["scores"] + 3 * k + 3)
                    pe.wait_ge(v_ready, 4 * (layer + 1))
                    pe.wait_ge(diag_done, s["scores"] + 3 * k + 3)
                    if k >= 1:
                        pe.wait_ge(osum_done, tr)
                    pe.matmul(bank[1][:, 0:3 * P], ones[:], diag[:, k % 2].rearrange("p g q -> p (g q)"), start=True, stop=True)
                cut = len(keys) // 2 - (len(keys) > 5)
                for m in (range(cut) if half == 0 else range(cut, len(keys))):
                    for pt in (pth, ptl):
                        last = pe.matmul(bank[0][:, 0:3 * P], v2[:, b, keys[m], kv * P:(kv + 1) * P], pt[:, k % 2, m, :],
                                         start=(m == 0 and pt is pth), stop=(m == len(keys) - 1 and pt is ptl))
                if half == 1:
                    last.then_inc(pv_done, 1)

            for i in range(len(tiles) + LAG + 2):
                if i == 2:
                    fourier()
                if i < len(tiles):
                    scores(i)
                if 0 <= i - LAG < len(tiles):
                    turn_probs(i - LAG)
                k, half = divmod(i - LAG - 3, 3)
                if 0 <= k < len(tiles) // 3 and half < 2:
                    weigh_values(k, half)
            r += len(tiles)
            ready = dict(zip((6, 0, 3), mix_counts(layer)))
            for d in range(W_OUT_TILES):
                slot_free(pe, r + d)
                pe.wait_ge(wlo_ready, t + d + 1)
                product(ring[(r + d) % 2], d % 2, KD, xh, xl, s["out_width"], order=[6, 7, 0, 1, 2, 3, 4, 5],
                        k_wait=(lambda k: pe.wait_ge(mix_ready, ready[k]) if k in ready else None) if d == 0 else None)

        @block.tensor
        def _(pe):
            def product(out, slot, nk, xs_hi, xs_lo, width, done=None, k_wait=None, order=None):
                order = order or list(range(nk))
                for i, k in enumerate(order):
                    if k_wait:
                        k_wait(k)
                    w_h, w_l = whi[:, slot, k * P:(k + 1) * P], wlo[:, slot, k * P:(k + 1) * P]
                    for m, (w, x) in enumerate(((w_h, xs_hi), (w_h, xs_lo), (w_l, xs_hi))):
                        for a, b in spans(width):
                            last = pe.matmul(out[:, a:b], w, x[:, k, a:b], start=(i == 0 and m == 0),
                                             stop=(i == nk - 1 and m == 2))
                last.then_inc(mm_done, 1)

            def product_pair(n, tt, width):
                for u in range(2):
                    pe.wait_ge(wlo_ready, tt + u + 1)
                for k in range(KD):
                    pe.wait_ge(x_ready, KD * n + k + 1)
                    for u in range(2):
                        w_h, w_l = whi[:, u, k * P:(k + 1) * P], wlo[:, u, k * P:(k + 1) * P]
                        for m, (w, x) in enumerate(((w_h, xh), (w_h, xl), (w_l, xh))):
                            for a, b in spans(width):
                                last = pe.matmul(ring[u][:, a:b], w, x[:, k, a:b], start=(k == 0 and m == 0),
                                                 stop=(k == KD - 1 and m == 2))
                        if k == KD - 1:
                            last.then_inc(mm_done, 1)

            def sum_chunks(n, width):
                pe.wait_ge(acc_done, (KD - 1) * (n + 1))
                for a, b in spans(width):
                    pe.matmul(side[:, a:b], ones[:], acc[:, a:b], start=True, stop=False)
                pe.wait_ge(sq_done, KD * (n + 1))
                for a, b in spans(width):
                    last = pe.matmul(side[:, a:b], ones[:], sq[:, (KD - 1) % 2, a:b], start=False, stop=True)
                last.then_inc(ssq_ready, 1)

            def ada_turn(u):
                pe.wait_ge(ada_lat_done, (u + 1) * KD)
                pe.wait_ge(ada_ctx_done, (u + 1) * KD)
                pe.wait_ge(ada_red_done, u * 4 + 2)
                for c in range(2):
                    for m in range(UC):
                        last = pe.transpose(bank[c][:, m * P:(m + 1) * P], ada_acc[:, c, m * P:(m + 1) * P], ident[:])
                last.then_inc(ada_turned, 1)

            pe.wait_ge(cond_ready, 1)
            pe.wait_ge(consts_ready, CONSTS)

            def turn_first(u):
                pe.wait_ge(ada_row_read, u + 1)
                for m in range(UC):
                    o = 2 * (UC * u + m)
                    last = pe.transpose(ring[1][:, o:o + 2], ada_rows[:, u % 2, m * P:(m + 1) * P], ident[0:2, 0:2])
                last.then_inc(first_turned, 1)

            for u in range(FIRST_UNITS):
                pe.wait_ge(ada_first_loaded[u % 4], 16 * (u // 4 + 1))
                if u >= 2:
                    pe.wait_ge(ada_row_read, u - 1)
                for k in range(KD):
                    last = pe.matmul(bank[u % 2][0:2, 0:ADA_COLS], scond[:, :, k], ada_first[u % 4][:, k], start=(k == 0),
                                     stop=(k == KD - 1))
                last.then_inc(ada_row_mm, 1)
                if u >= 1:
                    turn_first(u - 1)
            turn_first(FIRST_UNITS - 1)
            sum_chunks(0, TOK)

            for s in stages:
                layer, n, width, ow = s["layer"], s["n"], s["width"], s["out_width"]
                t, r = s["t"], s["r"]
                if s["kind"] == "mix":
                    pe_mixer(pe, s, product, product_pair)
                    sum_chunks(n + 1, ow)
                    continue

                def one(tt, slot):
                    pe.wait_ge(wlo_ready, tt + 1)
                    product(ring[slot], slot, KD, xh, xl, width)

                for g in range(GROUPS):
                    u0, nu = plan.ada.get((n, g), (0, 0))
                    slot_free(pe, r)
                    slot_free(pe, r + 1)
                    if g == 0:
                        product_pair(n, t, width)
                    else:
                        one(t, 0)
                        one(t + 1, 1)
                    if nu:
                        if u0 == 0:
                            for u in range(2):
                                slot_free(pe, r + u + 2)
                                one(t + u + 2, u)
                            ada_turn(0)
                        with pe.Fori(2 if u0 == 0 else 1, 1 + nu) as i:
                            for u in range(2):
                                slot_free(pe, r + u + 2, i, 1)
                                one(t + u + 2 * i, u)
                            ada_turn(i + (u0 - 1))
                    with pe.Fori(1 + nu, GF) as i:
                        for u in range(2):
                            slot_free(pe, r + u + 2 + 2 * nu, i, 1 + nu)
                            one(t + u + 2 * i, u)
                    t += 2 * GF
                    r += 2 * GF
                    a0 = s["pairs"] + g * GF

                    def down(tt, slot):
                        pe.wait_ge(wlo_ready, tt + 1)
                        product(ring[slot], slot, GF, ah, al, width,
                                k_wait=lambda k: pe.wait_ge(alo_done, a0 + max(k + 1, GF - 2)) if k == 0 or k >= GF - 2 else None)
                    for u in range(2):
                        slot_free(pe, r + u)
                        down(t + u, u)
                    with pe.Fori(1, KD // 2) as i:
                        for u in range(2):
                            slot_free(pe, r + u + 2, i, 1)
                            down(t + u + 2 * i, u)
                    t += KD
                    r += KD
                sum_chunks(n + 1, ow)

def columns_of_w_in():
    a_q, a_k, a_v, b_q, b_k, b_v, u = 0, 384, 512, 640, 1024, 1152, 1280
    head = lambda base, i: list(range(base + i * HD, base + (i + 1) * HD))
    run = lambda base: list(range(base, base + P))
    pairs = lambda base: [head(base, g) + head(base, g + 3) for g in range(3)]
    tiles = [run(b_k)] + pairs(b_q) + [run(a_k)] + pairs(a_q) + [run(a_v), run(b_v), run(u), run(u + P)]
    return [i for tile in tiles for i in tile]


def rows_of_w_out():
    head = lambda base, i: list(range(base + i * HD, base + (i + 1) * HD))
    rows = [i for base in (0, 384) for g in range(3) for i in head(base, g) + head(base, g + 3)]
    return rows + list(range(768, 1024))


def shape_constants():
    half = HD // 2
    inv = (ROPE_THETA ** (-np.arange(0, half, 2, dtype=np.float32) / half)).astype(np.float32)
    pos = np.arange(SEQ)
    p = np.arange(P) % HD
    place = np.where((p < half)[:, None], (pos // GRID_W)[None], (pos % GRID_W)[None]).astype(np.float32)
    angle = (place * inv[p % 16][:, None]).astype(np.float32).astype(np.float64)
    sign = np.where(p % half < 16, -1.0, 1.0)[:, None]
    rope = np.stack([np.cos(angle), np.sin(angle) * sign], 1).astype(np.float32)

    def dft(n):
        k = np.outer(np.arange(n), np.arange(n)) % n
        return np.cos(2 * np.pi * k / n) / np.sqrt(n), np.sin(2 * np.pi * k / n) / np.sqrt(n)

    cos, sin = dft(HD)
    chan = np.zeros((P, 2, P))
    for g in range(2):
        chan[g * HD:(g + 1) * HD, 0, g * HD:(g + 1) * HD] = cos
        chan[g * HD:(g + 1) * HD, 1, g * HD:(g + 1) * HD] = sin

    def positions(n):
        cos, sin = dft(n)
        return np.stack([cos, -sin]).reshape(2, n // P, P, n).transpose(2, 0, 1, 3)

    f = lambda a: np.ascontiguousarray(a, dtype=np.float32)
    return f(rope), f(chan), f(positions(SEQ)), f(positions(CTX))


def kernel(**inputs):
    import concourse.bacc as bacc
    from concourse.bass_utils import run_bass_kernel_spmd

    a = {k: np.ascontiguousarray(v) for k, v in inputs.items()}
    c = np.ascontiguousarray
    by_feature = lambda v: c(v.reshape(-1, P).T)
    tiles = lambda w, nt: c(w.reshape(DEPTH, -1, P, nt, P).transpose(0, 3, 2, 1, 4).reshape(DEPTH, nt, P, -1))
    gate_up = np.stack([np.stack([tiles(a[f"w{i}_gate"], NF), tiles(a[f"w{i}_up"], NF)], 2) for i in (1, 2)], 1)
    down = np.stack([a[f"w{i}_down"].reshape(DEPTH, GROUPS, GF, P, KD, P).transpose(0, 1, 4, 3, 2, 5) for i in (1, 2)], 1)
    rope, chan, lat, ctx = shape_constants()
    arrays = {
        "x_t": c(a["x"][0].reshape(SEQ, KD, P).transpose(2, 1, 0)),
        "ctx_t": c(a["ctx"][0].reshape(CTX, KD, P).transpose(2, 1, 0)),
        "c_cols": c(np.stack([by_feature(a["c"][0]), by_feature(a["c_ctx"])], 1)),
        "w_ada": c(a["w_ada"].reshape(DEPTH, KD, P, ADA_UNITS, ADA_COLS).transpose(0, 3, 2, 1, 4).reshape(DEPTH * ADA_UNITS, P, KD, ADA_COLS)),
        "b_ada": by_feature(a["b_ada"]),
        "gains": c(np.stack([a["g_ffn1"], a["g_mix"], a["g_ffn2"]], 1).reshape(DEPTH * 3, KD, P).transpose(2, 0, 1)),
        "g_final": by_feature(a["g_final"]),
        "qk_gain": c(np.tile(np.stack([a["g_qn"], a["g_kn"]], 1).reshape(DEPTH * 2, HD), (1, 2)).T),
        "sink": c(np.broadcast_to(a["sink"].reshape(1, -1), (P, DEPTH * 6))),
        "w_in": tiles(a["w_in"][:, :, columns_of_w_in()], W_IN_TILES),
        "w_four": a["w_four"],
        "w_out": tiles(a["w_out"][:, rows_of_w_out(), :], W_OUT_TILES),
        "w_gu": c(gate_up.reshape(2 * DEPTH, NF, 2, P, KD * P)),
        "w_down": c(down.reshape(2 * DEPTH, GROUPS, KD, P, GF * P)),
        "rope": rope, "dft_chan": chan, "dft_lat": lat, "dft_ctx": ctx,
    }
    nc = bacc.Bacc("TRN2", target_bir_lowering=False, num_devices=1)
    args = {k: nc.dram_tensor(k, v.shape, mybir.dt.from_np(v.dtype), kind="ExternalInput").ap() for k, v in arrays.items()}
    out = nc.dram_tensor("out", (P, KD, SEQ), F32, kind="ExternalOutput").ap()
    build(nc, out=out, **args)
    result = run_bass_kernel_spmd(nc, [arrays], core_ids=[0]).results[0]["out"]
    return c(result.transpose(2, 1, 0).reshape(1, SEQ, D_MODEL))
```
